# Optimizing a Trainium2 kernel written in Bass

```python
import math
import jax, jax.numpy as jnp
from jax import lax
import numpy as np

D_MODEL = 1024
BATCH = 1
SEQ = 256
DEPTH = 2

CHUNK = 64
Q_BLOCK = 128
EPS = 1e-6
A_HEADS = 4
A_QK_DIM = 32
A_V_DIM = 64
B_HEADS = 6
B_DIM = 64
CONV_WIDTH = 4
C_HEADS = 6
C_Q_LORA = 192
C_KV_LORA = 128
C_NOPE = 64
C_ROPE = 32
C_V_DIM = 64
ROPE_THETA = 10000.0
D_MIX = A_HEADS * A_V_DIM + B_HEADS * B_DIM + C_HEADS * C_V_DIM
IN_SIZES = (A_HEADS * A_QK_DIM, A_HEADS * A_QK_DIM, A_HEADS * A_QK_DIM, A_HEADS * A_QK_DIM, A_HEADS * A_V_DIM,
            B_HEADS * B_DIM, B_HEADS * B_DIM, B_HEADS * B_DIM, B_HEADS * B_DIM, B_HEADS, B_HEADS,
            C_Q_LORA, C_KV_LORA, C_ROPE)
IN_WIDTH = sum(IN_SIZES)
D_FF = 3584
N_EXPERTS = 8
TOP_K = 2
EXPERT_BLOCK = 256

kernel_name = "hybrid_hymba_diff_mlstm_mla_moe_block"

def rmsnorm(u, g):
    uf = u.astype(jnp.float32)
    r = uf * lax.rsqrt(jnp.mean(uf * uf, axis=-1, keepdims=True) + EPS)
    return (r * g.astype(jnp.float32)).astype(u.dtype)

def ada_modulation(c, w, b):
    p = jax.nn.silu(c) @ w + b
    shift, scale, gate = jnp.split(p, 3, axis=-1)
    return shift[:, None, :], scale[:, None, :], gate[:, None, :]

def chunk_mask(s0, s1):
    qc = (s0 + jnp.arange(s1 - s0)) // CHUNK
    kc = jnp.arange(s1) // CHUNK
    return kc[None, :] <= qc[:, None]

def masked_softmax(s, mask, scale):
    s = jnp.where(mask, s.astype(jnp.float32) * scale, -jnp.inf)
    return jax.nn.softmax(s, axis=-1)

def sweep_query_blocks(block_fn, seq):
    return jnp.concatenate([block_fn(s0, s0 + Q_BLOCK) for s0 in range(0, seq, Q_BLOCK)], axis=1)

def rope(u, cos, sin):
    half = u.shape[-1] // 2
    uf = u.astype(jnp.float32)
    u1, u2 = uf[..., :half], uf[..., half:]
    return jnp.concatenate([u1 * cos - u2 * sin, u1 * sin + u2 * cos], axis=-1).astype(u.dtype)

def causal_conv(u, w, b):
    k = w.shape[0]
    s = u.shape[1]
    up = jnp.pad(u, ((0, 0), (k - 1, 0), (0, 0)))
    return sum(up[:, j:j + s] * w[j] for j in range(k)) + b

def diff_attention_group(q1, q2, k1, k2, v, lam_q1, lam_k1, lam_q2, lam_k2, g_sub, lam_init):
    bsz, s, _ = q1.shape
    q1 = q1.reshape(bsz, s, A_HEADS, A_QK_DIM)
    q2 = q2.reshape(bsz, s, A_HEADS, A_QK_DIM)
    k1 = k1.reshape(bsz, s, A_HEADS, A_QK_DIM)
    k2 = k2.reshape(bsz, s, A_HEADS, A_QK_DIM)
    v = v.reshape(bsz, s, A_HEADS, A_V_DIM)
    f32 = jnp.float32
    lam = (jnp.exp(jnp.sum(lam_q1.astype(f32) * lam_k1.astype(f32)))
           - jnp.exp(jnp.sum(lam_q2.astype(f32) * lam_k2.astype(f32))) + lam_init)
    scale = A_QK_DIM ** -0.5

    def block(s0, s1):
        mask = chunk_mask(s0, s1)
        p1 = masked_softmax(jnp.einsum('bqhd,bkhd->bhqk', q1[:, s0:s1], k1[:, :s1]), mask, scale)
        p2 = masked_softmax(jnp.einsum('bqhd,bkhd->bhqk', q2[:, s0:s1], k2[:, :s1]), mask, scale)
        a = (p1 - lam * p2).astype(v.dtype)
        return jnp.einsum('bhqk,bkhd->bqhd', a, v[:, :s1])

    o = sweep_query_blocks(block, s)
    o = rmsnorm(o, g_sub) * (1.0 - lam_init)
    return o.reshape(bsz, s, A_HEADS * A_V_DIM)

def mlstm_group(q, k, v, o, ig_pre, fg_pre, w_conv, b_conv, b_i, b_f, g_out):
    bsz, s, _ = q.shape
    f32 = jnp.float32
    qk = jax.nn.silu(causal_conv(jnp.concatenate([q, k], axis=-1), w_conv, b_conv))
    q, k = jnp.split(qk, 2, axis=-1)
    nc = s // CHUNK

    def to_chunks(u):
        return u.astype(f32).reshape(bsz, nc, CHUNK, B_HEADS, B_DIM).transpose(1, 0, 3, 2, 4)

    def gate_chunks(g):
        return g.astype(f32).reshape(bsz, nc, CHUNK, B_HEADS).transpose(1, 0, 3, 2)

    qc, kc, vc = to_chunks(q), to_chunks(k) * (B_DIM ** -0.5), to_chunks(v)
    igc = gate_chunks(ig_pre.astype(f32) + b_i.astype(f32))
    lfc = jax.nn.log_sigmoid(gate_chunks(fg_pre.astype(f32) + b_f.astype(f32)))
    tril = jnp.tril(jnp.ones((CHUNK, CHUNK), dtype=bool))

    def step(carry, inp):
        cmat, nvec, m = carry
        qq, kk, vv, ig, lf = inp
        b = jnp.cumsum(lf, axis=-1)
        d = jnp.where(tril, b[..., :, None] - b[..., None, :] + ig[..., None, :], -jnp.inf)
        inter = b + m[..., None]
        m_t = jnp.maximum(inter, d.max(axis=-1))
        w_intra = jnp.exp(d - m_t[..., None])
        w_inter = jnp.exp(inter - m_t)
        sc = jnp.einsum('bhtd,bhsd->bhts', qq, kk) * w_intra
        num = jnp.einsum('bhts,bhsd->bhtd', sc, vv) + w_inter[..., None] * jnp.einsum('bhed,bhtd->bhte', cmat, qq)
        den = sc.sum(axis=-1) + w_inter * jnp.einsum('bhd,bhtd->bht', nvec, qq)
        h = num / jnp.maximum(jnp.abs(den), jnp.exp(-m_t))[..., None]
        b_last = b[..., -1]
        g = b_last[..., None] - b + ig
        m_new = jnp.maximum(b_last + m, g.max(axis=-1))
        w_s = jnp.exp(g - m_new[..., None])
        w_c = jnp.exp(b_last + m - m_new)
        cmat = w_c[..., None, None] * cmat + jnp.einsum('bhs,bhse,bhsd->bhed', w_s, vv, kk)
        nvec = w_c[..., None] * nvec + jnp.einsum('bhs,bhsd->bhd', w_s, kk)
        return (cmat, nvec, m_new), h

    init = (jnp.zeros((bsz, B_HEADS, B_DIM, B_DIM), f32), jnp.zeros((bsz, B_HEADS, B_DIM), f32),
            jnp.zeros((bsz, B_HEADS), f32))
    _, hc = lax.scan(step, init, (qc, kc, vc, igc, lfc))
    h = hc.transpose(1, 0, 3, 2, 4).reshape(bsz, s, B_HEADS, B_DIM)
    h = rmsnorm(h, g_out.reshape(B_HEADS, B_DIM)).reshape(bsz, s, B_HEADS * B_DIM)
    return h.astype(o.dtype) * jax.nn.sigmoid(o)

def mla_group(c_q, c_kv, k_rope, g_q_lat, g_kv_lat, w_uq, w_ukv, cos, sin):
    bsz, s, _ = c_q.shape
    q = (rmsnorm(c_q, g_q_lat) @ w_uq).reshape(bsz, s, C_HEADS, C_NOPE + C_ROPE)
    kv = (rmsnorm(c_kv, g_kv_lat) @ w_ukv).reshape(bsz, s, C_HEADS, C_NOPE + C_V_DIM)
    q_nope, q_rope = q[..., :C_NOPE], rope(q[..., C_NOPE:], cos[:, :, None, :], sin[:, :, None, :])
    k_nope, v = kv[..., :C_NOPE], kv[..., C_NOPE:]
    k_rope = rope(k_rope, cos, sin)
    scale = (C_NOPE + C_ROPE) ** -0.5

    def block(s0, s1):
        mask = chunk_mask(s0, s1)
        sc = (jnp.einsum('bqhd,bkhd->bhqk', q_nope[:, s0:s1], k_nope[:, :s1])
              + jnp.einsum('bqhr,bkr->bhqk', q_rope[:, s0:s1], k_rope[:, :s1]))
        p = masked_softmax(sc, mask, scale).astype(v.dtype)
        return jnp.einsum('bhqk,bkhd->bqhd', p, v[:, :s1])

    return sweep_query_blocks(block, s).reshape(bsz, s, C_HEADS * C_V_DIM)

def hybrid_mixer(h, positions, layer, w_in, w_out, lam_q1, lam_k1, lam_q2, lam_k2, g_diff,
                 w_conv, b_conv, b_igate, b_fgate, g_mlstm, g_q_lat, g_kv_lat, w_uq, w_ukv):
    split_idx = np.cumsum(IN_SIZES)[:-1].tolist()
    (q1, q2, k1, k2, va, qb, kb, vb, ob, ib, fb, cq, ckv, kr) = jnp.split(h @ w_in, split_idx, axis=-1)
    lam_init = 0.8 - 0.6 * math.exp(-0.3 * layer)
    out_a = diff_attention_group(q1, q2, k1, k2, va, lam_q1, lam_k1, lam_q2, lam_k2, g_diff, lam_init)
    out_b = mlstm_group(qb, kb, vb, ob, ib, fb, w_conv, b_conv, b_igate, b_fgate, g_mlstm)
    freqs = ROPE_THETA ** (-jnp.arange(0, C_ROPE, 2, dtype=jnp.float32) / C_ROPE)
    ang = positions.astype(jnp.float32)[..., None] * freqs
    out_c = mla_group(cq, ckv, kr, g_q_lat, g_kv_lat, w_uq, w_ukv, jnp.cos(ang), jnp.sin(ang))
    return jnp.concatenate([out_a, out_b, out_c], axis=-1) @ w_out

def swiglu(u, wg, wu, wd):
    return (jax.nn.silu(u @ wg) * (u @ wu)) @ wd

def moe_swiglu(h, w_router, b_router, w_gate_e, w_up_e, w_down_e):
    bsz, s, d = h.shape
    n = bsz * s
    t = h.reshape(n, d)
    logits = (t @ w_router).astype(jnp.float32) + b_router.astype(jnp.float32)
    top_val, top_idx = lax.top_k(logits, TOP_K)
    gates = jax.nn.softmax(top_val, axis=-1)
    e_flat = top_idx.reshape(-1)
    tok_flat = jnp.repeat(jnp.arange(n, dtype=jnp.int32), TOP_K)
    g_flat = gates.reshape(-1)
    order = jnp.argsort(e_flat, stable=True)
    e_sorted, tok_sorted, g_sorted = e_flat[order], tok_flat[order], g_flat[order]
    counts = jnp.zeros((N_EXPERTS,), jnp.int32).at[e_flat].add(1)
    starts = jnp.cumsum(counts) - counts
    padded = ((counts + EXPERT_BLOCK - 1) // EXPERT_BLOCK) * EXPERT_BLOCK
    pend = jnp.cumsum(padded)
    pstarts = pend - padded
    dest = pstarts[e_sorted] + (jnp.arange(n * TOP_K, dtype=jnp.int32) - starts[e_sorted])
    n_blocks = -(-(n * TOP_K) // EXPERT_BLOCK) + N_EXPERTS
    p = n_blocks * EXPERT_BLOCK
    buf_tok = jnp.full((p,), n, jnp.int32).at[dest].set(tok_sorted)
    t_pad = jnp.concatenate([t, jnp.zeros((1, d), t.dtype)], axis=0)
    xb = t_pad[buf_tok].reshape(n_blocks, EXPERT_BLOCK, d)
    blk_e = jnp.minimum(jnp.searchsorted(pend, jnp.arange(n_blocks) * EXPERT_BLOCK, side='right'), N_EXPERTS - 1)

    def expert_block(args):
        xblk, e = args
        return swiglu(xblk, w_gate_e[e], w_up_e[e], w_down_e[e])

    yb = lax.map(expert_block, (xb, blk_e)).reshape(p, d)
    y = jnp.zeros((n, d), h.dtype).at[tok_sorted].add(yb[dest] * g_sorted[:, None].astype(h.dtype))
    return y.reshape(bsz, s, d)

def setup_inputs(seed: int = 0) -> dict:
    key = jax.random.key(seed)
    ks = jax.random.split(key, 32)
    f32 = jnp.float32
    n_dense = (DEPTH + 1) // 2
    n_moe = DEPTH // 2

    def nrm(k, shape, scale):
        return jax.random.normal(k, shape, f32) * scale

    def gain(k, shape):
        return 1.0 + 0.05 * jax.random.normal(k, shape, f32)

    offsets = jax.random.randint(ks[2], (BATCH, 1), 0, 64, dtype=jnp.int32) * CHUNK
    positions = offsets + jnp.arange(SEQ, dtype=jnp.int32)[None, :]
    b_fgate = jnp.linspace(3.0, 6.0, B_HEADS, dtype=f32)[None, :] + 0.1 * jax.random.normal(ks[15], (DEPTH, B_HEADS), f32)
    return {
        "x": nrm(ks[0], (BATCH, SEQ, D_MODEL), 1.0),
        "c": nrm(ks[1], (BATCH, D_MODEL), 1.0),
        "positions": positions,
        "w_ada": nrm(ks[3], (DEPTH, 2, D_MODEL, 3 * D_MODEL), D_MODEL ** -0.5),
        "b_ada": nrm(ks[4], (DEPTH, 2, 3 * D_MODEL), 0.01),
        "g_norm": gain(ks[5], (DEPTH, 4, D_MODEL)),
        "w_in": nrm(ks[6], (DEPTH, D_MODEL, IN_WIDTH), D_MODEL ** -0.5),
        "w_out": nrm(ks[7], (DEPTH, D_MIX, D_MODEL), D_MIX ** -0.5),
        "lam_q1": nrm(ks[8], (DEPTH, A_QK_DIM), 0.1),
        "lam_k1": nrm(ks[9], (DEPTH, A_QK_DIM), 0.1),
        "lam_q2": nrm(ks[10], (DEPTH, A_QK_DIM), 0.1),
        "lam_k2": nrm(ks[11], (DEPTH, A_QK_DIM), 0.1),
        "g_diff": gain(ks[12], (DEPTH, A_V_DIM)),
        "w_conv": nrm(ks[13], (DEPTH, CONV_WIDTH, 2 * B_HEADS * B_DIM), CONV_WIDTH ** -0.5),
        "b_conv": nrm(ks[14], (DEPTH, 2 * B_HEADS * B_DIM), 0.01),
        "b_igate": nrm(ks[16], (DEPTH, B_HEADS), 0.1),
        "b_fgate": b_fgate,
        "g_mlstm": gain(ks[17], (DEPTH, B_HEADS * B_DIM)),
        "g_q_lat": gain(ks[18], (DEPTH, C_Q_LORA)),
        "g_kv_lat": gain(ks[19], (DEPTH, C_KV_LORA)),
        "w_uq": nrm(ks[20], (DEPTH, C_Q_LORA, C_HEADS * (C_NOPE + C_ROPE)), C_Q_LORA ** -0.5),
        "w_ukv": nrm(ks[21], (DEPTH, C_KV_LORA, C_HEADS * (C_NOPE + C_V_DIM)), C_KV_LORA ** -0.5),
        "w_gate_d": nrm(ks[22], (n_dense, D_MODEL, D_FF), D_MODEL ** -0.5),
        "w_up_d": nrm(ks[23], (n_dense, D_MODEL, D_FF), D_MODEL ** -0.5),
        "w_down_d": nrm(ks[24], (n_dense, D_FF, D_MODEL), D_FF ** -0.5),
        "w_router": nrm(ks[25], (n_moe, D_MODEL, N_EXPERTS), D_MODEL ** -0.5),
        "b_router": nrm(ks[26], (n_moe, N_EXPERTS), 0.01),
        "w_gate_e": nrm(ks[27], (n_moe, N_EXPERTS, D_MODEL, D_FF), D_MODEL ** -0.5),
        "w_up_e": nrm(ks[28], (n_moe, N_EXPERTS, D_MODEL, D_FF), D_MODEL ** -0.5),
        "w_down_e": nrm(ks[29], (n_moe, N_EXPERTS, D_FF, D_MODEL), D_FF ** -0.5),
    }

def reference(x, c, positions, w_ada, b_ada, g_norm, w_in, w_out, lam_q1, lam_k1, lam_q2, lam_k2, g_diff,
              w_conv, b_conv, b_igate, b_fgate, g_mlstm, g_q_lat, g_kv_lat, w_uq, w_ukv,
              w_gate_d, w_up_d, w_down_d, w_router, b_router, w_gate_e, w_up_e, w_down_e):
    for l in range(DEPTH):
        shift, scale, gate = ada_modulation(c, w_ada[l, 0], b_ada[l, 0])
        h = rmsnorm(x, g_norm[l, 0]) * (1.0 + scale) + shift
        y = hybrid_mixer(h, positions, l, w_in[l], w_out[l], lam_q1[l], lam_k1[l], lam_q2[l], lam_k2[l], g_diff[l],
                         w_conv[l], b_conv[l], b_igate[l], b_fgate[l], g_mlstm[l], g_q_lat[l], g_kv_lat[l],
                         w_uq[l], w_ukv[l])
        x = x + gate * rmsnorm(y, g_norm[l, 1])
        shift, scale, gate = ada_modulation(c, w_ada[l, 1], b_ada[l, 1])
        h = rmsnorm(x, g_norm[l, 2]) * (1.0 + scale) + shift
        if l % 2 == 0:
            y = swiglu(h, w_gate_d[l // 2], w_up_d[l // 2], w_down_d[l // 2])
        else:
            y = moe_swiglu(h, w_router[l // 2], b_router[l // 2], w_gate_e[l // 2], w_up_e[l // 2], w_down_e[l // 2])
        x = x + gate * rmsnorm(y, g_norm[l, 3])
    return x


_drawn_inputs = setup_inputs


def setup_inputs(seed=0):
    import zlib

    import numpy as np

    out = dict(_drawn_inputs(seed))
    spreads = {}
    factors = {'b_conv': 8.0, 'b_igate': 64.0, 'g_q_lat': 7.019, 'b_router': 8.0}
    for name, (base, spread) in spreads.items():
        noise = np.random.default_rng([zlib.crc32(name.encode()), seed]).standard_normal(out[name].shape)
        drawn = base * np.exp(spread * noise) if base else spread * noise
        out[name] = __import__('jax').numpy.asarray(drawn.astype(out[name].dtype))
    for name, factor in factors.items():
        out[name] = (out[name] * factor).astype(out[name].dtype)
    return out
```

```python
from contextlib import ExitStack

import numpy as np

import concourse.bass as bass
from concourse import mybir

F32 = mybir.dt.float32
I32 = mybir.dt.int32
U32 = mybir.dt.uint32
ALU = mybir.AluOpType
ACT = mybir.ActivationFunctionType
AX = mybir.AxisListType

P = 128
T, D, L = 256, 1024, 2
TB = T // P
KD = D // P
CHUNK, EPS = 64, 1e-6
AH, AQ, AV = 4, 32, 64
BH, BD, CW = 6, 64, 4
CH, CQL, CKV, CN, CR, CV = 6, 192, 128, 64, 32, 64
FF, NE = 3584, 8
NEG = -1.0e30
COL_Q, COL_VA, COL_QK, COL_VB, COL_OB, COL_LAT = 0, 512, 768, 1536, 1920, 2304
IN_W = 2668
LATW = IN_W - COL_LAT
LAM0 = [0.8 - 0.6 * float(np.exp(-0.3 * l)) for l in range(L)]
SC_A, SC_B, SC_C = AQ ** -0.5, BD ** -0.5, (CN + CR) ** -0.5

ARENA = 24096
SLOTS, SW = 7, 256
FT = FF // P
STAGES = FT // 2
USES = 3 * STAGES
NVAR = (128, 192, 256)

C_ID, C_TRI, C_CAUS, C_MU, C_MK, C_IOTA, C_ROT, C_FREQ, C_END = 0, 128, 256, 384, 512, 640, 896, 928, 929
TWO_PI = 2.0 * np.pi
PI_1 = 6.28125
PI_2 = float(np.float32(np.floor((TWO_PI - PI_1) * 2 ** 22) / 2 ** 22))
PI_3 = float(np.float32(TWO_PI - PI_1 - PI_2))
PI_LOW = 3.1415925


def const_table():
    t = np.zeros((P, C_END), np.float32)
    i = np.arange(P)
    t[:, C_ID:C_ID + P] = np.eye(P)
    t[:, C_TRI:C_TRI + P] = i[:, None] < i[None, :]
    t[:, C_CAUS:C_CAUS + P] = np.where(i[:, None] <= i[None, :], 0.0, NEG)
    t[:, C_MU:C_MU + P] = i[None, :] < CHUNK
    t[:, C_MK:C_MK + P] = np.where(i[None, :] < CHUNK, 0.0, NEG)
    t[:, C_IOTA:C_IOTA + T] = np.arange(T)
    for m in range(CR // 2):
        t[CN + CR // 2 + m, C_ROT + m] = -1.0
        t[CN + m, C_ROT + CR // 2 + m] = 1.0
    f = (10000.0 ** (-np.arange(0, CR, 2) / CR)).astype(np.float32)
    t[CN:CN + CR, C_FREQ] = np.concatenate([f, f])
    return t


def weight_uses():
    uses = []

    def ada(batch):
        uses.extend(("ada", n, 4 * g + c) for n, g in batch for c in range(4))

    def mixer(l):
        for c, w in W_IN_ORDER:
            uses.append(("in", l, (c, w)))
        ada(ADA_MIXER[l])
        uses.extend(("out", l, c) for c in range(D // SW))

    ada(ADA_START)
    mixer(0)
    for s in range(STAGES):
        uses.extend([("gate", 0, s), ("up", 0, s)])
        if s % 2:
            ada([ADA_DENSE[s // 2]])
        uses.append(("down", 0, s))
    mixer(1)
    return uses


W_IN_ORDER = [(COL_LAT, 256), (COL_LAT + 256, LATW - 256), (COL_Q, 256), (COL_Q + 256, 256), (COL_VA, 256),
              (COL_QK, 256), (COL_QK + 256, 256), (COL_QK + 512, 256), (COL_OB, 256), (COL_OB + 256, 128),
              (COL_VB, 256), (COL_VB + 256, 128)]
ADA_START = [(0, 0), (0, 1)]
ADA_MIXER = [[(0, 2), (1, 0), (1, 1)], []]
ADA_DENSE = [(1, 2)] + [(n, g) for n in (2, 3) for g in range(3)]
IN_ITEM = dict(zip(W_IN_ORDER, ["lat1", "lat1", "a0", "a1", "va", "qk0", "qk1", "qk2", "ob0", "ob1", "vb1", "vb1"]))
PJ_LAYER = ["lat0", "lat1", "a0", "a1", "va", "qk0", "uq0", "uq1", "uq2", "uk0", "uk1", "uk2", "uv0", "uv1",
            "qk1", "qk2", "ob0", "ob1", "vb0", "vb1"]
SC_LAYER = ([("a", u) for u in range(8)] + [("rot", i) for i in range(4)] + [("c", u) for u in range(6)]
            + [(k, h) for h in range(BH) for k in ("w", "s")])
TR_LAYER = (["lx", "lz", "lf", "at0", "at1", "at2", "at3", "ao"] + [f"pt{u}" for u in range(6)]
            + ["gt", "co0", "co1", "bo0", "bo1", "ada", "mt0", "mt1", "mt2", "mt3"])


class Ring:

    def __init__(self, names, n):
        self.at = {name: i for i, name in enumerate(names)}
        assert len(self.at) == len(names)
        self.n = n

    def bank(self, name):
        return self.at[name] % self.n

    def full(self, name):
        return self.at[name] + 1

    def before(self, name):
        return self.at[name] // self.n


ROW_SLOT = {x: i % 2 for i, x in enumerate(ADA_START + ADA_MIXER[0] + ADA_DENSE + ADA_MIXER[1])}


def ada_steps(n):
    steps = [(0, j) for j in range(min(n, 2))]
    for j in range(n):
        steps.append((1, j))
        if j + 2 < n:
            steps.append((0, j + 2))
    return steps


def tr_names():
    def ada(batch):
        return [(("ada", "adat")[i], *batch[j]) for i, j in ada_steps(len(batch))]

    def norm(kind, n):
        return [(kind, n, step) for step in ("partial", "total", "laid")]

    names = ["param1", "param2", "lam"] + ada(ADA_START)
    for l in range(L):
        names += norm("pre", 2 * l)
        for x in TR_LAYER:
            names += ada(ADA_MIXER[l]) if x == "ada" else [(x, l)]
        names += norm("post", 2 * l) + norm("pre", 2 * l + 1)
        if l == 0:
            names += sum((ada([x]) for x in ADA_DENSE), [])
            names += norm("post", 1)
    names += ["router", "rank"] + norm("post", 3)
    return names


def rs_names():
    names = []
    for l in range(L):
        names += [("pre", 2 * l), ("c", l), ("a", l), ("b", l), ("post", 2 * l), ("pre", 2 * l + 1), ("post", 2 * l + 1)]
    return names


def build(nc, ap, out):
    uses = weight_uses()
    n_before = len(uses)
    slot_of = [u % SLOTS for u in range(n_before + USES)]
    assert USES % SLOTS == 0
    use_at = {u: i for i, u in enumerate(uses)}
    PJ = Ring([(x, l) for l in range(L) for x in PJ_LAYER], 2)
    SC = Ring([(x, l) for l in range(L) for x in SC_LAYER], 4)
    TR = Ring(tr_names(), 2)
    MS = {name: i for i, name in enumerate([(kind, l) for l in range(L) for kind in "cab"])}
    RS = {name: i for i, name in enumerate(rs_names())}

    with ExitStack() as ctx:
        def sb(name, shape, dt=F32):
            return ctx.enter_context(nc.sbuf_tensor(name, shape, dt))

        def ps(name, shape):
            return ctx.enter_context(nc.psum_tensor(name, shape, F32))

        def sem(name):
            return ctx.enter_context(nc.semaphore(name))

        Y = ps("Y", [P, 4, 512])
        PG = ps("PG", [P, 2, 512])
        TRB = ps("TRB", [P, 2, 512])
        pj = [Y[:, 0, :], Y[:, 1, :]]
        sc = [Y[:, 2, :], Y[:, 3, :], PG[:, 0, :], PG[:, 1, :]]
        tr = [TRB[:, 0, :], TRB[:, 1, :]]
        Yf = Y[:, :, :].rearrange("p b c -> p (b c)")
        Yk = Yf.rearrange("p (k t) -> p k t", k=KD)

        ring = sb("ring", [P, SLOTS, KD, SW])
        xT = sb("xT", [P, KD, T])
        hT = sb("hT", [P, KD, T])
        scr = sb("scr", [P, KD, T])
        tok = sb("tok", [P, TB, D])
        mixT = sb("mixT", [P, KD, T])
        con = sb("con", [P, C_END])
        ones = sb("ones", [P, P])
        pcol = sb("pcol", [P, 2, P])
        ccol = sb("ccol", [P, KD, 32])
        s4 = sb("s4", [P, T])
        arow = sb("arow", [P, 2, SW])
        prow = arow[:, :, 0:P]
        meps = sb("meps", [P, TB])
        root_ = sb("root_", [P, TB])
        diag = sb("diag", [P, TB, P])
        mod = sb("mod", [P, 2 * L, 24])
        gs = sb("gs", [P, 2 * L, KD])
        gg = sb("gg", [P, 2 * L, KD])
        lam_in = sb("lam_in", [AQ, 4, L])
        lam_pr = sb("lam_pr", [AQ, 2, L])
        lam_e = sb("lam_e", [P, 2, L])
        lam_v = sb("lam_v", [P, L, 2])
        gq = sb("gq", [P, L, 2])
        gdr = sb("gdr", [P, L])
        gd = sb("gd", [P, L])
        bg = sb("bg", [BH, L, 2])
        rbias = sb("rbias", [P, NE])
        wr = sb("wr", [P, KD, NE])
        ms = sb("ms", [P, 3 * L, 12])
        rs = sb("rs", [P, 3 * L, 12])
        half = sb("half", [P, 12])
        rsb = sb("rsb", [P, T])
        cos = sb("cos", [P, T])
        sin = sb("sin", [P, T])
        posi = sb("posi", [P, T], I32)
        ss = sb("ss", [P, 4])
        red = sb("red", [P, 12])
        den = sb("den", [P, 12])
        rden = sb("rden", [P, 12])
        aK = sb("aK", [P, 12])
        em = sb("em", [P, 12])
        nm = sb("nm", [P, 14, 2])
        se = sb("se", [P, 14, 2])
        rc = sb("rc", [P, 14, 2])

        arena = sb("arena", [P, ARENA])
        cnt = sb("cnt", [P, NE], I32)
        ix8 = sb("ix8", [P, TB, NE], U32)
        top = {"mixer": 0, "ffn": 0}

        def cut(user, *dims):
            n = int(np.prod(dims))
            a = arena[:, top[user]:top[user] + n]
            top[user] += n
            return shaped(a, *dims)

        def shaped(a, *dims):
            if len(dims) == 2:
                a = a.rearrange("p (a b) -> p a b", a=dims[0])
            if len(dims) == 3:
                a = a.rearrange("p (a b c) -> p a b c", a=dims[0], b=dims[1])
            return a

        wuq = cut("mixer", 2, CH * (CN + CR))
        wukv = cut("mixer", CH * (CN + CV))
        qkA = cut("mixer", 4, T)
        va = cut("mixer", TB, AH * AV)
        lat_at = top["mixer"]
        lat = cut("mixer", TB, LATW)
        latn = cut("mixer", TB, 352)
        cqT = cut("mixer", T)
        ckT = cut("mixer", T)
        zT = cut("mixer", T)
        qall = cut("mixer", CH, T)
        kall = cut("mixer", CH, T)
        vc = cut("mixer", TB, CH * CV)
        E = cut("mixer", 4, 2 * T)
        aA = cut("mixer", 2, 3 * P)
        aT = cut("mixer", AH, 3 * P)
        conv_at = top["mixer"]
        raw = cut("mixer", 6, T + CW - 1)
        cv = cut("mixer", 6, T)
        PT = cut("mixer", CH // 2, 6 * P)
        vbx = cut("mixer", TB, BH, BD + 1)
        sqj = cut("mixer", 3 * T)
        g_i, g_f, g_n, g_e, g_a, g_m, g_b = (cut("mixer", T) for _ in range(7))
        obt = shaped(arena[:, lat_at:lat_at + 3 * T], 3, T)
        qcos = shaped(PT.rearrange("p a b -> p (a b)")[:, 0:(CH + 1) * T], CH + 1, T)
        scw = shaped(arena[:, conv_at:conv_at + BH * 3 * P], BH, 3 * P)
        W = shaped(arena[:, conv_at + BH * 3 * P:conv_at + (BH + 2) * 3 * P], 2, 3 * P)
        hb = shaped(E.rearrange("p a b -> p (a b)")[:, 0:TB * BH * BD], TB * BH, BD)
        scrf = scr[:, :, :].rearrange("p k t -> p (k t)")
        qks = scr[:, 0:6, :]
        kro = scr[:, 6, :]
        act = cut("ffn", 2, T)
        sg = cut("ffn", 2, T)
        yacc = cut("ffn", KD, T)
        yeT = cut("ffn", KD, T)
        yeK = cut("ffn", TB, D)
        oh = cut("ffn", TB, T)
        ohg = cut("ffn", TB, T)
        gPT = cut("ffn", TB, T)
        lg = cut("ffn", TB, NE)
        mx8 = cut("ffn", TB, NE)
        ixf = cut("ffn", TB, NE)
        gt2 = cut("ffn", TB, 4)
        oh1 = cut("ffn", TB, NE)
        oh2 = cut("ffn", TB, NE)
        Gm = cut("ffn", TB, NE)
        Mm = cut("ffn", TB, NE)
        pos = cut("ffn", TB, NE)
        assert max(top.values()) <= ARENA, top

        ident = con[:, C_ID:C_ID + P]
        tri = con[:, C_TRI:C_TRI + P]
        caus = con[:, C_CAUS:C_CAUS + P]
        iota = con[:, C_IOTA:C_IOTA + T]

        gn = pcol[:, 0, 0:64].rearrange("p (l s k) -> p l s k", l=L, s=4)
        wc = pcol[:, 0, 64:112].rearrange("p (l j i) -> p l j i", l=L, j=CW)
        bc = pcol[:, 0, 112:124].rearrange("p (l i) -> p l i", l=L)
        bada = pcol[:, 1, 0:96].rearrange("p (n k) -> p n k", n=2 * L)
        craw = pcol[:, 1, 96:104]
        gml = pcol[:, 1, 104:110].rearrange("p (l i) -> p l i", l=L)
        gkv = pcol[:, 1, 110:112]

        rows1 = [(0, 64, ap["g_norm"].rearrange("l s (k p) -> (l s k) p", p=P)),
                 (64, 112, ap["w_conv"].rearrange("l j (k p) -> (l j k) p", p=P)),
                 (112, 124, ap["b_conv"].rearrange("l (k p) -> (l k) p", p=P))]
        rows2 = [(0, 96, ap["b_ada"].rearrange("l s (k p) -> (l s k) p", p=P)),
                 (96, 104, ap["c"].rearrange("b (k p) -> (b k) p", p=P)),
                 (104, 110, ap["g_mlstm"].rearrange("l (k p) -> (l k) p", p=P)),
                 (110, 112, ap["g_kv_lat"])]
        params = [(con[:, :], ap["consts"])]
        params += [(prow[a:b, i, :], src) for i, rows_ in enumerate((rows1, rows2)) for a, b, src in rows_]
        params += [(lam_in[:, i, :], ap[name].rearrange("l d -> d l"))
                   for i, name in enumerate(("lam_q1", "lam_q2", "lam_k1", "lam_k2"))]
        params += [(gdr[i * AV:(i + 1) * AV, :], ap["g_diff"].rearrange("l d -> d l")) for i in range(2)]
        params += [(gq[:, :, 0], ap["g_q_lat"][:, 0:P].rearrange("l d -> d l")),
                   (gq[0:CQL - P, :, 1], ap["g_q_lat"][:, P:CQL].rearrange("l d -> d l")),
                   (bg[:, :, 0], ap["b_igate"].rearrange("l h -> h l")),
                   (bg[:, :, 1], ap["b_fgate"].rearrange("l h -> h l")),
                   (rbias[:, :], ap["b_router"].to_broadcast([P, NE])),
                   (wr[:, :, :], ap["w_router"][0].rearrange("(k p) e -> p k e", p=P)),
                   (posi[CN:CN + CR, :], ap["positions"].to_broadcast([CR, T]))]
        n_param = len(params)

        param_in = sem("param_in")
        x_in = sem("x_in")
        wl_in = sem("wl_in")
        landed = [sem(f"landed{i}") for i in range(SLOTS)]
        out_read = sem("out_read")
        const_set = sem("const_set")
        pj_full = sem("pj_full")
        pj_free = [sem(f"pj_free{i}") for i in range(2)]
        sc_full = sem("sc_full")
        sc_free = [sem(f"sc_free{i}") for i in range(4)]
        tr_full = sem("tr_full")
        tr_free = [sem(f"tr_free{i}") for i in range(2)]
        y_full = sem("y_full")
        diag_ready = sem("diag_ready")
        y_quarter = sem("y_quarter")
        sq_ready = sem("sq_ready")
        mean_ready = sem("mean_ready")
        rstd_ready = sem("rstd_ready")
        hx_ready = sem("hx_ready")
        h_ready = sem("h_ready")
        upd_ready = sem("upd_ready")
        x_upd = sem("x_upd")
        ccol_ready = sem("ccol_ready")
        mod_ready = sem("mod_ready")
        lam_prod = sem("lam_prod")
        rope_in = sem("rope_in")
        rope_set = sem("rope_set")
        dve_seq = sem("dve_seq")
        act_seq = sem("act_seq")
        pool_seq = sem("pool_seq")
        latn_ready = sem("latn_ready")
        kr_ready = sem("kr_ready")
        gate_in = sem("gate_in")
        gate_exp = sem("gate_exp")
        gate_ln = sem("gate_ln")
        gates_ready = sem("gates_ready")
        conv_ready = sem("conv_ready")
        qks_ready = sem("qks_ready")
        obt_tanh = sem("obt_tanh")
        obt_ready = sem("obt_ready")
        qcos_ready = sem("qcos_ready")
        rope_done = sem("rope_done")
        negmax = sem("negmax")
        combined = sem("combined")
        ao_sq = sem("ao_sq")
        hb_sq = sem("hb_sq")
        tok_ready = sem("tok_ready")
        gu_full = sem("gu_full")
        silu_done = sem("silu_done")
        act_ready = sem("act_ready")
        down_done = sem("down_done")
        gap_ready = sem("gap_ready")
        gap_exp = sem("gap_exp")
        routed = sem("routed")
        htok_ready = sem("htok_ready")
        hot_ready = sem("hot_ready")
        ax_full = sem("ax_full")
        ax_free = [sem(f"ax_free{i}") for i in range(2)]
        ye_ready = sem("ye_ready")
        yacc_zero = sem("yacc_zero")
        yacc_ready = sem("yacc_ready")
        out_ready = sem("out_ready")
        out_done = sem("out_done")

        AX_T, AX_F = 14, 7

        def use_wait(eng, u):
            eng.wait_ge(landed[slot_of[u]], 16 * (u // SLOTS + 1))

        def per_bank(n):
            return 4 if n <= P else 2

        def ye(n, k):
            q = per_bank(n)
            return Y[:, k // q, (k % q) * n:(k % q + 1) * n]

        def variants(eng, n, emit):
            with eng.If(n > NVAR[1]):
                emit(NVAR[2])
            with eng.Else():
                with eng.If(n > NVAR[0]):
                    emit(NVAR[1])
                with eng.Else():
                    emit(NVAR[0])

        def ye_half(copy_, n, h):
            if n <= P:
                o = yeT[:, 4 * h:4 * h + 4, 0:n]
                i_ = Y[:, h, 0:4 * n].rearrange("p (k t) -> p k t", k=4)
            elif n == 192:
                o = yeT[:, 4 * h:4 * h + 4, 0:n].rearrange("p (b q) t -> p b q t", b=2)
                i_ = Y[:, 2 * h:2 * h + 2, 0:2 * n].rearrange("p b (q t) -> p b q t", q=2)
            else:
                o = yeT[:, 4 * h:4 * h + 4, 0:n]
                i_ = Yk[:, 4 * h:4 * h + 4, :]
            copy_(o, i_).then_inc(ye_ready, 1)

        def blocks(n):
            return [(j, min(P, n - j * P)) for j in range((n + P - 1) // P)]

        def pj_done(name, l):
            return pj_free[PJ.bank((name, l))], PJ.before((name, l)) + 1

        def sc_done(kind, i, l):
            name = ((kind, i), l)
            return sc_free[SC.bank(name)], SC.before(name) + 1

        def tr_done(*name):
            name = name if len(name) > 1 else name[0]
            return tr_free[TR.bank(name)], TR.before(name) + 1

        tr_before_experts = [TR.before(x) + 1 for x in ("router", "rank")]
        if TR.bank("router"):
            tr_before_experts.reverse()

        block = ctx.enter_context(nc.Block())

        @block.sync
        def _(sp):
            w_in, w_out = ap["w_in"], ap["w_out"]

            def cols(w, c, n):
                return w[:, c:c + n].rearrange("(k p) c -> p k c", p=P)

            def rows(w, s):
                return w[s * 2 * P:(s + 1) * 2 * P, :].rearrange("(f p) c -> p f c", p=P)

            def last_reader(kind, a, b):
                if kind == "ada":
                    return tr_full, TR.full(("ada", a, b // 4))
                if kind == "in":
                    return pj_full, PJ.full((IN_ITEM[b], a))
                if kind == "out":
                    return (y_full, 2 + a) if b == D // SW - 1 else (out_read, (D // SW - 1) * a + b + 1)
                return (down_done if kind == "down" else gu_full), 2 * b + 2

            for u, (kind, a, b) in enumerate(uses):
                if u >= SLOTS:
                    sp.wait_ge(*last_reader(*uses[u - SLOTS]))
                slot = ring[:, slot_of[u], :, :]
                if kind == "ada":
                    src = cols(ap["w_ada"][a // 2, a % 2], b * SW, SW)
                elif kind == "in":
                    src = cols(w_in[a], b[0], b[1])
                    slot = slot[:, :, 0:b[1]]
                elif kind == "out":
                    src = cols(w_out[a], b * SW, SW)
                elif kind == "gate":
                    src = cols(ap["w_gate_d"][0], b * SW, SW)
                elif kind == "up":
                    src = cols(ap["w_up_d"][0], b * SW, SW)
                else:
                    src = rows(ap["w_down_d"][0], b)
                    slot = slot.rearrange("p k c -> p (k c)").rearrange("p (f c) -> p f c", f=2)
                sp.dma_start(slot, src).then_inc(landed[slot_of[u]], 16)

            wge = ap["w_gate_e"].rearrange("l e d f -> (l e d) f")
            wue = ap["w_up_e"].rearrange("l e d f -> (l e d) f")
            wde = ap["w_down_e"].rearrange("l e f d -> (l e f) d")
            sp.wait_ge(y_full, 3)
            with sp.Fori(0, NE) as e:
                for i in range(USES):
                    s, kind = i // 3, i % 3
                    ps_, pk = (i - SLOTS) % USES // 3, (i - SLOTS) % 3
                    sp.wait_ge(down_done if pk == 2 else gu_full,
                               e * FT + ((FT if i >= SLOTS else 0) + 2 * ps_ + 2))
                    slot = ring[:, slot_of[n_before + i], :, :]
                    if kind < 2:
                        src = (wge, wue)[kind][bass.ds(e * D, D), s * SW:(s + 1) * SW].rearrange("(k p) c -> p k c", p=P)
                    else:
                        src = wde[bass.ds(e * FF + s * 2 * P, 2 * P), :].rearrange("(f p) c -> p f c", p=P)
                        slot = slot.rearrange("p k c -> p (k c)").rearrange("p (f c) -> p f c", f=2)
                    sp.dma_start(slot, src).then_inc(landed[slot_of[n_before + i]], 16)
            sp.wait_ge(out_ready, 4)
            sp.dma_start(out[0].rearrange("(b p) d -> p b d", p=P), tok[:, :, :]).then_inc(out_done, 16)
            sp.wait_ge(out_done, 16)

        @block.tensor
        def _(pe):
            mm = nc.tensor.matmul

            def take_pj(name):
                b = PJ.bank(name)
                if PJ.before(name):
                    pe.wait_ge(pj_free[b], PJ.before(name))
                return pj[b]

            def take_sc(name):
                b = SC.bank(name)
                if SC.before(name):
                    pe.wait_ge(sc_free[b], SC.before(name))
                return sc[b]

            def take_tr(name):
                b = TR.bank(name)
                if TR.before(name):
                    pe.wait_ge(tr_free[b], TR.before(name))
                return tr[b]

            def stats(kind, n, q):
                bank = take_tr((kind, n, "partial"))
                for k in range(KD):
                    if k % 2 == 0:
                        pe.wait_ge(sq_ready, 4 * q + k // 2 + 1)
                    g = 32 * (k % 4)
                    last = mm(bank[g:g + 32, 0:T], ones[:, 0:32], scr[:, k, :], start=(k < 4), stop=(k >= 4))
                last.then_inc(tr_full, 1)
                bank = take_tr((kind, n, "total"))
                pe.wait_ge(*tr_done(kind, n, "partial"))
                for b in range(TB):
                    last = mm(bank[:, b:b + 1], s4[:, b * P:(b + 1) * P], ones[:, 0:1], start=True, stop=True)
                last.then_inc(tr_full, 1)
                bank = take_tr((kind, n, "laid"))
                pe.wait_ge(diag_ready, q + 1)
                for b in range(TB):
                    last = mm(bank[:, b * P:(b + 1) * P], ones[:, :], diag[:, b, :], start=True, stop=True)
                last.then_inc(tr_full, 1)

            def ada_rows(n, g):
                bank = take_tr(("ada", n, g))
                us = [use_at[("ada", n, 4 * g + c)] for c in range(4)]
                for u in us:
                    use_wait(pe, u)
                for k in range(KD):
                    for c, u in enumerate(us):
                        last = mm(bank[32 * c:32 * c + 32, 0:SW], ccol[:, k, :], ring[:, slot_of[u], k, :],
                                  start=(k == 0), stop=(k == KD - 1))
                last.then_inc(tr_full, 1)

            def ada_columns(n, g):
                bank = take_tr(("adat", n, g))
                pe.wait_ge(*tr_done("ada", n, g))
                for j in range(2):
                    last = nc.tensor.transpose(bank[:, j * P:(j + 1) * P], arow[:, ROW_SLOT[n, g], j * P:(j + 1) * P], ident)
                last.then_inc(tr_full, 1)

            def ada(batch):
                for i, j in ada_steps(len(batch)):
                    (ada_rows, ada_columns)[i](*batch[j])

            def gu_tile(n, slots, half, tile, e=None):
                bank = PG[:, tile % 2, :]
                rhs = hT if e is None else mixT
                for m in range(2):
                    for k in range(KD):
                        last = mm(bank[:, m * T:m * T + n], ring[:, slots[m], k, half * P:(half + 1) * P],
                                  rhs[:, k, 0:n], start=(k == 0), stop=(k == KD - 1))
                return last

            def down_tile(n, slot, half, tile, view):
                w = ring[:, slot, :, :].rearrange("p k c -> p (k c)").rearrange("p (f c) -> p f c", f=2)
                q = per_bank(n)
                for k in range(KD):
                    last = mm(view(k), w[:, half, k * P:(k + 1) * P], act[:, tile % 2, 0:n],
                              start=(tile == 0 and k % q == 0), stop=(tile == FT - 1), skip_group_check=True)
                return last

            def mixer(l):
                def slot(name, c):
                    u = use_at[(name, l, c)]
                    use_wait(pe, u)
                    return slot_of[u]

                def fm(bank_part, s, c, m):
                    for k in range(KD):
                        last = mm(bank_part, ring[:, s, k, c:c + m], hT[:, k, :], start=(k == 0), stop=(k == KD - 1))
                    return last

                def tm(bank_part, s, b, m):
                    for k in range(KD):
                        last = mm(bank_part, hT[:, k, b * P:(b + 1) * P], ring[:, s, k, 0:m],
                                  start=(k == 0), stop=(k == KD - 1))
                    return last

                def fm_pair(name, key, n=2):
                    bank = take_pj((name, l))
                    s = slot("in", key)
                    for i in range(n):
                        last = fm(bank[:, i * T:(i + 1) * T], s, i * P, P)
                    last.then_inc(pj_full, 1)
                    return last

                def a_unit(h, b):
                    u = 2 * h + b
                    bank = take_sc((("a", u), l))
                    keys = (b + 1) * P
                    r = slice(AQ * h, AQ * (h + 1))
                    for j in range(2):
                        mm(bank[:, j * T:j * T + keys], qkA[r, j, b * P:(b + 1) * P], qkA[r, 2 + j, 0:keys],
                           start=True, stop=False)
                        last = mm(bank[:, j * T + b * P:j * T + keys], con[AQ * h:AQ * h + 1, C_MU:C_MU + P],
                                  con[AQ * h:AQ * h + 1, C_MK:C_MK + P], start=False, stop=True)
                    last.then_inc(sc_full, 1)

                def c_unit(u):
                    p, b = u // 2, u % 2
                    bank = take_sc((("c", u), l))
                    keys = (b + 1) * P
                    for j in range(2):
                        mm(bank[:, j * T:j * T + keys], qall[0:CN + CR, 2 * p + j, b * P:(b + 1) * P],
                           kall[0:CN + CR, 2 * p + j, 0:keys], start=True, stop=False)
                        last = mm(bank[:, j * T + b * P:j * T + keys], con[0:1, C_MU:C_MU + P],
                                  con[0:1, C_MK:C_MK + P], start=False, stop=True)
                    last.then_inc(sc_full, 1)

                def at(h):
                    bank = take_tr((f"at{h}", l))
                    pe.wait_ge(combined, AH * l + h + 1)
                    for i in range(3):
                        last = nc.tensor.transpose(bank[:, i * P:(i + 1) * P], aA[:, h % 2, i * P:(i + 1) * P], ident)
                    last.then_inc(tr_full, 1)

                def pt(u):
                    p, b = u // 2, u % 2
                    bank = take_tr((f"pt{u}", l))
                    pe.wait_ge(*sc_done("c", u, l))
                    for j in range(2):
                        for kb in range(b + 1):
                            i = j * (b + 1) + kb
                            last = nc.tensor.transpose(bank[:, i * P:(i + 1) * P],
                                                       E[:, u % 4, j * T + kb * P:j * T + (kb + 1) * P], ident)
                    last.then_inc(tr_full, 1)

                pe.wait_ge(h_ready, KD * (2 * l + 1))
                keys = W_IN_ORDER
                s0, s1 = slot("in", keys[0]), slot("in", keys[1])
                for b in range(TB):
                    bank = take_pj((f"lat{b}", l))
                    tm(bank[:, 0:SW], s0, b, SW)
                    last = tm(bank[:, SW:LATW], s1, b, LATW - SW)
                    last.then_inc(pj_full, 1)
                fm_pair("a0", keys[2])
                fm_pair("a1", keys[3])
                bank = take_pj(("va", l))
                s = slot("in", keys[4])
                for b in range(TB):
                    last = tm(bank[:, b * T:(b + 1) * T], s, b, SW)
                last.then_inc(pj_full, 1)
                bank = take_tr(("lx", l))
                pe.wait_ge(latn_ready, l + 1)
                pe.wait_ge(kr_ready, l + 1)
                for i in range(2):
                    for b in range(TB):
                        last = nc.tensor.transpose(bank[:, i * T + b * P:i * T + (b + 1) * P],
                                                   latn[:, b, i * P:(i + 1) * P], ident)
                last.then_inc(tr_full, 1)
                bank = take_tr(("lz", l))
                for b in range(TB):
                    nc.tensor.transpose(bank[0:96, b * P:(b + 1) * P], latn[:, b, 256:352], ident)
                    last = nc.tensor.transpose(bank[0:BH, T + b * P:T + (b + 1) * P], lat[:, b, 0:BH], ident)
                last.then_inc(tr_full, 1)
                bank = take_tr(("lf", l))
                for b in range(TB):
                    last = nc.tensor.transpose(bank[0:BH, b * P:(b + 1) * P], lat[:, b, BH:2 * BH], ident)
                last.then_inc(tr_full, 1)
                fm_pair("qk0", keys[5])
                pe.wait_ge(*pj_done("a0", l))
                pe.wait_ge(*pj_done("a1", l))
                a_unit(0, 0)
                a_unit(0, 1)
                pe.wait_ge(*tr_done("lx", l))
                pe.wait_ge(*tr_done("lz", l))
                pe.wait_ge(wl_in, 48 * (l + 1))
                for p in range(3):
                    bank = take_pj((f"uq{p}", l))
                    for j in range(2):
                        c = (2 * p + j) * (CN + CR)
                        mm(bank[0:96, j * T:(j + 1) * T], wuq[:, 0, c:c + 96], cqT[:, :], start=True, stop=False)
                        last = mm(bank[0:96, j * T:(j + 1) * T], wuq[0:64, 1, c:c + 96], zT[0:64, :],
                                  start=False, stop=True)
                    last.then_inc(pj_full, 1)
                for p in range(3):
                    bank = take_pj((f"uk{p}", l))
                    for j in range(2):
                        c = (2 * p + j) * (CN + CV)
                        last = mm(bank[0:CN, j * T:(j + 1) * T], wukv[:, c:c + CN], ckT[:, :], start=True, stop=True)
                    last.then_inc(pj_full, 1)
                wv = wukv.rearrange("p (h c) -> p h c", h=CH)[:, :, CN:CN + CV]
                for b in range(TB):
                    bank = take_pj((f"uv{b}", l))
                    last = mm(bank[:, 0:CH * CV].rearrange("p (h c) -> p h c", h=CH), ckT[:, b * P:(b + 1) * P], wv,
                              start=True, stop=True)
                    last.then_inc(pj_full, 1)
                a_unit(1, 0)
                a_unit(1, 1)
                fm_pair("qk1", keys[6])
                for h in range(2, AH):
                    for b in range(TB):
                        a_unit(h, b)
                fm_pair("qk2", keys[7])
                rot = con[CN:CN + CR, C_ROT:C_ROT + CR]
                pe.wait_ge(*pj_done("uq1", l))
                pe.wait_ge(*pj_done("uq2", l))
                for i in range(4):
                    bank = take_sc((("rot", i), l))
                    src = qall[CN:CN + CR, 2 * i:2 * i + 2, :].rearrange("p h t -> p (h t)") if i < 3 else zT[CN:CN + CR, :]
                    n = 2 * T if i < 3 else T
                    mm(bank[CN:CN + CR, 0:n], rot, src, start=True, stop=True).then_inc(sc_full, 1)
                at(0)
                at(1)
                fm_pair("ob0", keys[8])
                fm_pair("ob1", keys[9], 1)
                at(2)
                at(3)
                pe.wait_ge(rope_done, l + 1)
                pe.wait_ge(*pj_done("uk1", l))
                pe.wait_ge(*pj_done("uk2", l))
                pe.wait_ge(*sc_done("rot", 2, l))
                for u in range(4):
                    c_unit(u)
                bank = take_tr(("ao", l))
                pe.wait_ge(*tr_done("at2", l))
                pe.wait_ge(*tr_done("at3", l))
                pe.wait_ge(*pj_done("va", l))
                for b in range(TB):
                    for h in range(AH):
                        o = bank[:, (b * AH + h) * AV:(b * AH + h + 1) * AV]
                        for kb in range(b + 1):
                            last = mm(o, aT[:, h, (b + kb) * P:(b + kb + 1) * P], va[:, kb, h * AV:(h + 1) * AV],
                                      start=(kb == 0), stop=(kb == b))
                last.then_inc(tr_full, 1)
                s0, s1 = slot("in", keys[10]), slot("in", keys[11])
                for b in range(TB):
                    bank = take_pj((f"vb{b}", l))
                    tm(bank[:, 0:SW], s0, b, SW)
                    tm(bank[:, SW:SW + P], s1, b, P).then_inc(pj_full, 1)
                pt(0)
                c_unit(4)
                pt(1)
                c_unit(5)
                for u in range(2, 6):
                    pt(u)
                bank = take_tr(("gt", l))
                pe.wait_ge(gates_ready, l + 1)
                for i, g in enumerate((g_a, g_b)):
                    for b in range(TB):
                        c = (i * TB + b) * BH
                        last = nc.tensor.transpose(bank[:, c:c + BH], g[0:BH, b * P:(b + 1) * P], ident[0:BH, 0:BH])
                last.then_inc(tr_full, 1)
                pe.wait_ge(qks_ready, l + 1)
                for h in range(BH):
                    bank = take_sc((("w", h), l))
                    sel = ident[0:BH, h:h + 1].to_broadcast([BH, P])
                    mm(bank[:, 0:T], sel, g_m[0:BH, :], start=True, stop=False, skip_group_check=True)
                    mm(bank[:, T:T + P], sel, g_m[0:BH, P:T], start=False, stop=False, skip_group_check=True)
                    mm(bank[:, 0:P], ident, caus, start=False, stop=False, skip_group_check=True)
                    mm(bank[:, T:T + P], ident, caus, start=False, stop=True,
                       skip_group_check=True).then_inc(sc_full, 1)
                    bank = take_sc((("s", h), l))
                    r = slice(BD * (h % 2), BD * (h % 2) + BD)
                    mm(bank[:, 0:T], qks[r, 3 + h // 2, 0:P], qks[r, h // 2, :], start=True, stop=True)
                    mm(bank[:, T:T + P], qks[r, 3 + h // 2, P:T], qks[r, h // 2, P:T],
                       start=True, stop=True).then_inc(sc_full, 1)
                pe.wait_ge(*tr_done("pt4", l))
                pe.wait_ge(*tr_done("pt5", l))
                pe.wait_ge(*pj_done("uv0", l))
                pe.wait_ge(*pj_done("uv1", l))
                for b in range(TB):
                    bank = take_tr((f"co{b}", l))
                    for h in range(CH):
                        for kb in range(b + 1):
                            c = (2 * b + (h % 2) * (b + 1) + kb) * P
                            last = mm(bank[:, h * CV:(h + 1) * CV], PT[:, h // 2, c:c + P],
                                      vc[:, kb, h * CV:(h + 1) * CV], start=(kb == 0), stop=(kb == b))
                    last.then_inc(tr_full, 1)
                pe.wait_ge(*sc_done("s", BH - 2, l))
                pe.wait_ge(*sc_done("s", BH - 1, l))
                pe.wait_ge(*pj_done("vb0", l))
                pe.wait_ge(*pj_done("vb1", l))
                for b in range(TB):
                    bank = take_tr((f"bo{b}", l))
                    for h in range(BH):
                        o = bank[:, h * (BD + 1):(h + 1) * (BD + 1)]
                        for kb in range(b + 1):
                            c = kb * T if kb == b else P
                            last = mm(o, scw[:, h, c:c + P], vbx[:, kb, h, :], start=(kb == 0), stop=(kb == b))
                    last.then_inc(tr_full, 1)
                ada(ADA_MIXER[l])
                for i in range(4):
                    bank = take_tr((f"mt{i}", l))
                    if i == 0:
                        pe.wait_ge(tok_ready, l + 1)
                    for j in range(2):
                        for b in range(TB):
                            f = 2 * i + j
                            last = nc.tensor.transpose(bank[:, j * T + b * P:j * T + (b + 1) * P],
                                                       tok[:, b, f * P:(f + 1) * P], ident)
                    last.then_inc(tr_full, 1)
                pe.wait_ge(*tr_done("mt2", l))
                pe.wait_ge(*tr_done("mt3", l))
                for b in range(2):
                    pe.wait_ge(pj_free[b], len(PJ_LAYER) // 2 * (l + 1))
                for b in range(4):
                    pe.wait_ge(sc_free[b], len([i for i in range(len(SC_LAYER) * (l + 1)) if i % 4 == b]))
                for c in range(D // SW):
                    s = slot("out", c)
                    for j in range(2):
                        for k in range(KD):
                            last = mm(Yk[:, 2 * c + j, :], ring[:, s, k, j * P:(j + 1) * P], mixT[:, k, :],
                                      start=(k == 0), stop=(k == KD - 1))
                    last.then_inc(out_read if c < D // SW - 1 else y_full, 1)

            pe.wait_ge(param_in, 16 * n_param)
            pe.wait_ge(const_set, 3)
            for i, (name, m) in enumerate((("param1", 124), ("param2", 112))):
                bank = take_tr(name)
                nc.tensor.transpose(bank[:, 0:m], prow[0:m, i, :], ident[0:m, 0:m]).then_inc(tr_full, 1)
            bank = take_tr("lam")
            pe.wait_ge(lam_prod, 2)
            mm(bank[:, 0:2 * L], ones[0:AQ, :], lam_pr[:, :, :].rearrange("p a l -> p (a l)"),
               start=True, stop=True).then_inc(tr_full, 1)
            pe.wait_ge(x_in, 16)
            for k in range(KD):
                for b in range(TB):
                    last = nc.tensor.transpose(Yk[:, k, b * P:(b + 1) * P], tok[:, b, k * P:(k + 1) * P], ident)
            last.then_inc(y_full, 1)
            pe.wait_ge(ccol_ready, 1)
            ada(ADA_START)

            stats("pre", 0, 0)
            mixer(0)
            stats("post", 0, 1)
            stats("pre", 1, 2)
            pe.wait_ge(h_ready, 2 * KD)
            for t in range(FT + 1):
                if t < FT:
                    s, half = t // 2, t % 2
                    us = [use_at[("gate", 0, s)], use_at[("up", 0, s)]]
                    for u in us:
                        use_wait(pe, u)
                    if t >= 2:
                        pe.wait_ge(act_ready, t - 1)
                    gu_tile(T, [slot_of[u] for u in us], half, t).then_inc(gu_full, 1)
                if t % 4 == 3:
                    ada_columns(*ADA_DENSE[t // 4])
                if t >= 1:
                    s, half = (t - 1) // 2, (t - 1) % 2
                    u = use_at[("down", 0, s)]
                    use_wait(pe, u)
                    pe.wait_ge(act_ready, t)
                    down_tile(T, slot_of[u], half, t - 1, lambda k: Yk[:, k, :]).then_inc(down_done, 1)
                if t % 4 == 2:
                    ada_rows(*ADA_DENSE[t // 4])
            stats("post", 1, 3)

            stats("pre", 2, 4)
            mixer(1)
            stats("post", 2, 5)
            stats("pre", 3, 6)
            pe.wait_ge(h_ready, 4 * KD)
            bank = take_tr("router")
            for b in range(TB):
                for k in range(KD):
                    last = mm(bank[:, b * NE:(b + 1) * NE], hT[:, k, b * P:(b + 1) * P], wr[:, k, :],
                              start=(k == 0), stop=(k == KD - 1))
            last.then_inc(tr_full, 1)
            for k in range(KD):
                for b in range(TB):
                    last = nc.tensor.transpose(Y[:, 2 * b + k // 4, (k % 4) * P:(k % 4 + 1) * P],
                                               hT[:, k, b * P:(b + 1) * P], ident)
            last.then_inc(y_full, 1)
            bank = take_tr("rank")
            pe.wait_ge(routed, 1)
            mm(bank[:, 0:NE], tri, Mm[:, 0, :], start=True, stop=True)
            mm(bank[:, NE:2 * NE], ones[:, :], Mm[:, 0, :], start=True, stop=False)
            mm(bank[:, NE:2 * NE], tri, Mm[:, 1, :], start=False, stop=True)
            mm(bank[:, 2 * NE:3 * NE], ones[:, :], Mm[:, 0, :], start=True, stop=False)
            mm(bank[:, 2 * NE:3 * NE], ones[:, :], Mm[:, 1, :], start=False, stop=True).then_inc(tr_full, 1)
            pe.wait_ge(htok_ready, 4)
            for b in range(2):
                pe.wait_ge(tr_free[b], tr_before_experts[b])

            for b in range(2):
                pe.sem_inc(ax_free[b], AX_F)
            with pe.Fori(0, NE) as e:
                n_tok = pe.value_load(cnt[0:1, bass.ds(e, 1)], min_val=0, max_val=T)

                def expert(n):
                    ax = [0]

                    def take():
                        i = ax[0]
                        ax[0] += 1
                        pe.wait_ge(ax_free[i % 2], e * AX_F + (AX_F + i // 2))
                        return tr[i % 2]

                    pe.wait_ge(hot_ready, e * 1 + 1)
                    for i in range(4):
                        bank = take()
                        for j in range(2):
                            k = 2 * i + j
                            for b in range(TB):
                                last = mm(bank[:, j * T:j * T + n], tok[:, b, k * P:(k + 1) * P], oh[:, b, 0:n],
                                          start=(b == 0), stop=(b == TB - 1))
                        last.then_inc(ax_full, 1)
                    for b in range(TB):
                        bank = take()
                        for j, m in blocks(n):
                            last = nc.tensor.transpose(bank[:, j * P:(j + 1) * P], ohg[:, b, j * P:(j + 1) * P], ident)
                        last.then_inc(ax_full, 1)
                    for b in range(2):
                        pe.wait_ge(ax_free[b], e * AX_F + (AX_F + 2))
                    for t in range(FT + 1):
                        if t < FT:
                            s, half = t // 2, t % 2
                            us = [n_before + 3 * s + m for m in range(2)]
                            if half == 0:
                                for u in us:
                                    pe.wait_ge(landed[slot_of[u]], e * (16 * USES // SLOTS) + 16 * (u // SLOTS + 1))
                            pe.wait_ge(act_ready, e * FT + (FT + t - 1))
                            gu_tile(n, [slot_of[u] for u in us], half, t, e).then_inc(gu_full, 1)
                        if t >= 1:
                            s, half = (t - 1) // 2, (t - 1) % 2
                            u = n_before + 3 * s + 2
                            if half == 0:
                                pe.wait_ge(landed[slot_of[u]], e * (16 * USES // SLOTS) + 16 * (u // SLOTS + 1))
                            pe.wait_ge(act_ready, e * FT + (FT + t))
                            down_tile(n, slot_of[u], half, t - 1, lambda k: ye(n, k)).then_inc(down_done, 1)
                    for i in range(4):
                        bank = take()
                        if i == 0:
                            pe.wait_ge(ye_ready, e * 2 + 2)
                        for j, m in blocks(n):
                            for q in range(2):
                                last = nc.tensor.transpose(bank[:, (2 * j + q) * P:(2 * j + q + 1) * P],
                                                           yeT[:, 2 * i + q, j * P:(j + 1) * P], ident)
                        last.then_inc(ax_full, 1)
                    for b in range(2):
                        pe.wait_ge(ax_free[b], e * AX_F + (AX_F + 5))
                    for i in range(4):
                        bank = take()
                        bl = blocks(n)
                        for q in range(2):
                            k = 2 * i + q
                            for j, m in bl:
                                last = mm(bank[:, q * T:(q + 1) * T], yeK[0:m, j, k * P:(k + 1) * P], gPT[0:m, j, :],
                                          start=(j == 0), stop=(j == len(bl) - 1))
                        last.then_inc(ax_full, 1)
                    assert ax[0] == AX_T

                variants(pe, n_tok, expert)

            for b in range(2):
                pe.wait_ge(ax_free[b], (NE + 1) * AX_F)
            stats("post", 3, 7)
            pe.wait_ge(x_upd, 4 * KD)
            for k in range(KD):
                for b in range(TB):
                    last = nc.tensor.transpose(Y[:, 2 * b + k // 4, (k % 4) * P:(k % 4 + 1) * P],
                                               xT[:, k, b * P:(b + 1) * P], ident)
            last.then_inc(y_full, 1)

        @block.scalar
        def _(act_e):
            ae = act_e

            def run(out_, in_, func, **kw):
                return nc.scalar.activation(out_, in_, func, **kw)

            def load_latent_weights(l):
                ae.dma_start(wuq[:, 0, :], ap["w_uq"][l, 0:P, :]).then_inc(wl_in, 16)
                ae.dma_start(wuq[0:CQL - P, 1, :], ap["w_uq"][l, P:CQL, :]).then_inc(wl_in, 16)
                ae.dma_start(wukv, ap["w_ukv"][l]).then_inc(wl_in, 16)

            def squares_pre(n):
                for j in range(4):
                    if n == 0:
                        ae.wait_ge(y_quarter, j + 1)
                    else:
                        ae.wait_ge(x_upd, KD * (n - 1) + 2 * j + 2)
                    run(scr[:, 2 * j:2 * j + 2, :], xT[:, 2 * j:2 * j + 2, :], ACT.Square).then_inc(sq_ready, 1)

            def shift(n):
                for k in range(KD):
                    ae.wait_ge(hx_ready, KD * n + k + 1)
                    run(hT[:, k, :], hT[:, k, :], ACT.Identity, bias=mod[:, n, k:k + 1]).then_inc(h_ready, 1)

            def squares_post(n, ready, value):
                ae.wait_ge(ready, value)
                for j in range(4):
                    src = yacc[:, 2 * j:2 * j + 2, :] if n == 3 else Yk[:, 2 * j:2 * j + 2, :]
                    run(scr[:, 2 * j:2 * j + 2, :], src, ACT.Square).then_inc(sq_ready, 1)

            def ada_rows(n, g):
                name = ("ada", n, g)
                ae.wait_ge(tr_full, TR.full(name))
                run(arow[:, ROW_SLOT[n, g], :], tr[TR.bank(name)][:, 0:SW], ACT.Copy).then_inc(tr_free[TR.bank(name)], 1)

            def mixer(l):
                def pj_item(name):
                    ae.wait_ge(pj_full, PJ.full((name, l)))
                    return pj[PJ.bank((name, l))], pj_free[PJ.bank((name, l))]

                def tr_item(name):
                    ae.wait_ge(tr_full, TR.full((name, l)))
                    return tr[TR.bank((name, l))], tr_free[TR.bank((name, l))]

                def exps(kind, u):
                    i = u if kind == "a" else 8 + u
                    ae.wait_ge(negmax, 14 * l + i + 1)
                    if kind == "a" and u >= 4:
                        ae.wait_ge(combined, AH * l + (u - 4) // 2 + 1)
                    if kind == "c" and u < 4:
                        ae.wait_ge(combined, AH * l + (u + 4) // 2 + 1)
                    if kind == "c" and u >= 4:
                        ae.wait_ge(tr_full, TR.full((f"pt{u - 4}", l)))
                    name = ((kind, u), l)
                    bank, keys = sc[SC.bank(name)], (u % 2 + 1) * P
                    for j in range(2):
                        last = run(E[:, i % 4, j * T:j * T + keys], bank[:, j * T:j * T + keys], ACT.Exp,
                                   bias=nm[:, i, j:j + 1], accum_out=se[:, i, j:j + 1])
                    last.then_inc(sc_free[SC.bank(name)], 1)

                for b in range(TB):
                    bank, free = pj_item(f"lat{b}")
                    run(lat[:, b, :], bank[:, 0:LATW], ACT.Copy)
                    o = 3 * P * b
                    run(sqj[:, o:o + CQL], bank[:, 12:12 + CQL], ACT.Square, scale=CQL ** -0.5, accum_out=ss[:, b:b + 1])
                    run(sqj[:, o + CQL:o + CQL + CKV], bank[:, 12 + CQL:12 + CQL + CKV], ACT.Square,
                        scale=CKV ** -0.5, accum_out=ss[:, 2 + b:3 + b]).then_inc(free, 1)
                bank, free = pj_item("a0")
                run(qkA[:, 0:2, :], bank.rearrange("p (a t) -> p a t", a=2), ACT.Copy, scale=SC_A).then_inc(free, 1)

                def raw_pair(i):
                    bank, free = pj_item(f"qk{i}")
                    run(raw[:, 2 * i:2 * i + 2, CW - 1:], bank.rearrange("p (a t) -> p a t", a=2), ACT.Copy).then_inc(free, 1)

                raw_pair(0)
                exps("a", 0)
                exps("a", 1)
                for p in range(3):
                    bank, free = pj_item(f"uq{p}")
                    run(qall[0:96, 2 * p:2 * p + 2, :], bank[0:96, :].rearrange("p (a t) -> p a t", a=2), ACT.Copy,
                        scale=SC_C).then_inc(free, 1)
                exps("a", 2)
                exps("a", 3)
                raw_pair(1)
                ae.wait_ge(gate_in, l + 1)
                run(g_e[0:BH, :], g_n[0:BH, :], ACT.Exp).then_inc(gate_exp, 1)
                ae.wait_ge(gate_exp, l + 1)
                run(g_e[0:BH, :], g_e[0:BH, :], ACT.Ln, bias=1.0).then_inc(gate_ln, 1)
                for u in range(4, 8):
                    exps("a", u)
                raw_pair(2)

                def at(h):
                    bank, free = tr_item(f"at{h}")
                    run(aT[:, h, :], bank[:, 0:3 * P], ACT.Copy).then_inc(free, 1)

                at(0)
                at(1)
                bank, free = pj_item("ob0")
                run(obt[:, 0:2, :], bank.rearrange("p (a t) -> p a t", a=2), ACT.Copy).then_inc(free, 1)
                bank, free = pj_item("ob1")
                run(obt[:, 2, :], bank[:, 0:T], ACT.Copy).then_inc(free, 1)
                at(2)
                at(3)
                ae.wait_ge(conv_ready, l + 1)
                run(qks, cv, ACT.Silu).then_inc(qks_ready, 1)
                ae.wait_ge(*pj_done("ob0", l))
                ae.wait_ge(*pj_done("ob1", l))
                run(obt, obt, ACT.Tanh, scale=0.5).then_inc(obt_tanh, 1)
                for u in range(4):
                    exps("c", u)
                bank = tr[TR.bank(("ao", l))]
                ae.wait_ge(tr_full, TR.full(("ao", l)))
                run(sqj[:, 0:2 * T], bank, ACT.Square).then_inc(ao_sq, 1)

                def pt(u):
                    p, b = u // 2, u % 2
                    bank, free = tr_item(f"pt{u}")
                    o, n = 2 * b * P, 2 * (b + 1) * P
                    run(PT[:, p, o:o + n], bank[:, 0:n], ACT.Copy).then_inc(free, 1)

                pt(0)
                exps("c", 4)
                exps("c", 5)
                pt(2)
                pt(4)
                bank, free = tr_item("gt")
                run(aK[:, :], bank[:, 0:12], ACT.Copy)
                run(em[:, :], bank[:, 12:24], ACT.Exp).then_inc(free, 1)
                ae.wait_ge(*tr_done("gt", l))
                for h in range(BH):
                    name = (("w", h), l)
                    bank = sc[SC.bank(name)]
                    ae.wait_ge(sc_full, SC.full(name))
                    if h >= 2:
                        ae.wait_ge(*sc_done("s", h - 2, l))
                    run(W[:, h % 2, 0:T], bank[:, 0:T], ACT.Exp, bias=aK[:, h:h + 1])
                    run(W[:, h % 2, T:T + P], bank[:, T:T + P], ACT.Exp,
                        bias=aK[:, BH + h:BH + h + 1]).then_inc(sc_free[SC.bank(name)], 1)
                ae.wait_ge(*tr_done("bo0", l))
                ae.wait_ge(*tr_done("bo1", l))
                run(sqj[:, 0:2 * BH * BD].rearrange("p (a d) -> p a d", d=BD), hb, ACT.Square).then_inc(hb_sq, 1)
                for n, g in ADA_MIXER[l]:
                    ada_rows(n, g)
                bank, free = tr_item("mt0")
                run(mixT[:, 0:2, :], bank.rearrange("p (a t) -> p a t", a=2), ACT.Copy, scale=gd[:, l:l + 1]).then_inc(free, 1)
                bank, free = tr_item("mt3")
                run(mixT[:, 6:8, :], bank.rearrange("p (a t) -> p a t", a=2), ACT.Copy).then_inc(free, 1)

            with nc.allow_non_contiguous_dma(reason="a few hundred single parameters, once"):
                for dst, src in params:
                    ae.dma_start(dst, src).then_inc(param_in, 16)
            ae.dma_start(tok[:, :, :], ap["x"][0].rearrange("(b p) d -> p b d", p=P)).then_inc(x_in, 16)
            load_latent_weights(0)
            ae.wait_ge(*tr_done("param2"))
            ae.wait_ge(const_set, 3)
            run(ccol[:, :, 0], craw, ACT.Silu).then_inc(ccol_ready, 1)
            ae.wait_ge(rope_in, 2)
            run(sin[CN:CN + CR, :], sin[CN:CN + CR, :], ACT.Sin).then_inc(rope_set, 1)
            run(cos[CN:CN + CR, :], cos[CN:CN + CR, :], ACT.Sin).then_inc(rope_set, 1)
            ae.wait_ge(tr_full, TR.full("lam"))
            run(lam_e[:, :, :], tr[TR.bank("lam")][:, 0:2 * L].rearrange("p (a l) -> p a l", a=2),
                ACT.Exp).then_inc(tr_free[TR.bank("lam")], 1)
            ae.wait_ge(y_full, 1)
            for j in range(4):
                run(xT[:, 2 * j:2 * j + 2, :], Yk[:, 2 * j:2 * j + 2, :], ACT.Copy).then_inc(y_quarter, 1)

            for n, g in ADA_START:
                ada_rows(n, g)
            squares_pre(0)
            shift(0)
            mixer(0)
            squares_post(0, y_full, 2)
            squares_pre(1)
            shift(1)
            for t in range(FT):
                ae.wait_ge(gu_full, t + 1)
                if t >= 2:
                    ae.wait_ge(act_ready, t - 1)
                run(sg[:, t % 2, :], PG[:, t % 2, 0:T], ACT.Silu).then_inc(silu_done, 1)
                if t % 4 == 2:
                    ada_rows(*ADA_DENSE[t // 4])
            squares_post(1, down_done, FT)
            load_latent_weights(1)
            squares_pre(2)
            shift(2)
            mixer(1)
            squares_post(2, y_full, 3)
            squares_pre(3)
            shift(3)
            ae.wait_ge(y_full, 4)
            for q in range(4):
                run(tok[:, q // 2, (q % 2) * 512:(q % 2 + 1) * 512], Y[:, q, :], ACT.Copy).then_inc(htok_ready, 1)
            ae.wait_ge(gap_ready, 1)
            run(gt2[:, :, 1], gt2[:, :, 0], ACT.Exp).then_inc(gap_exp, 1)
            ae.wait_ge(*tr_done("rank"))
            ae.wait_ge(yacc_zero, 2)
            with ae.Fori(0, NE) as e:
                n_tok = ae.value_load(cnt[0:1, bass.ds(e, 1)], min_val=0, max_val=T)

                def expert(n):
                    def item(i):
                        ae.wait_ge(ax_full, e * AX_T + (i + 1))
                        return tr[i % 2]

                    for i in (0, 2):
                        bank = item(i)
                        run(mixT[:, 2 * i:2 * i + 2, 0:n], bank.rearrange("p (a t) -> p a t", a=2)[:, :, 0:n],
                            ACT.Copy).then_inc(ax_free[0], 1)
                    bank = item(4)
                    for j, m in blocks(n):
                        last = run(gPT[0:m, j, 0:P], bank[0:m, j * P:(j + 1) * P], ACT.Copy)
                    last.then_inc(ax_free[0], 1)
                    for t in range(FT):
                        ae.wait_ge(gu_full, e * FT + (FT + t + 1))
                        ae.wait_ge(act_ready, e * FT + (FT + t - 1))
                        run(sg[:, t % 2, 0:n], PG[:, t % 2, 0:n], ACT.Silu).then_inc(silu_done, 1)
                    ae.wait_ge(down_done, e * FT + 2 * FT)
                    ye_half(run_copy, n, 0)
                    for i in (6, 8):
                        bank = item(i)
                        for j, m in blocks(n):
                            c = 2 * (i - 6) * P
                            last = run(yeK[0:m, j, c:c + T], bank[0:m, j * T:(j + 1) * T], ACT.Copy)
                        last.then_inc(ax_free[0], 1)

                def run_copy(o, i_):
                    return run(o, i_, ACT.Copy)

                variants(ae, n_tok, expert)
            squares_post(3, yacc_ready, 4 * NE)
            ae.wait_ge(y_full, 5)
            for q in range(4):
                run(tok[:, q // 2, (q % 2) * 512:(q % 2 + 1) * 512], Y[:, q, :], ACT.Copy).then_inc(out_ready, 1)

        @block.vector
        def _(ve):
            V = nc.vector
            steps = [0]

            def mark(ins):
                ins.then_inc(dve_seq, 1)
                steps[0] += 1
                return ins

            def settle():
                ve.wait_ge(dve_seq, steps[0])

            def tr_item(*name):
                name = name if len(name) > 1 else name[0]
                ve.wait_ge(tr_full, TR.full(name))
                return tr[TR.bank(name)], tr_free[TR.bank(name)]

            def root(name):
                ve.wait_ge(rstd_ready, RS[name] + 1)
                return rs[:, MS[name], :]

            def mean(kind, n):
                bank, free = tr_item(kind, n, "partial")
                V.tensor_copy(s4[:, :], bank[:, 0:T]).then_inc(free, 1)
                bank, free = tr_item(kind, n, "total")
                V.tensor_scalar(meps[:, :], bank[:, 0:TB], 1.0 / (32 * D), EPS, ALU.mult, ALU.add).then_inc(free, 1)
                ve.wait_ge(rstd_ready, RS[(kind, n)] + 1)
                for b in range(TB):
                    last = V.tensor_scalar(diag[:, b, :], ident, root_[:, b:b + 1], None, ALU.mult)
                last.then_inc(diag_ready, 1)
                bank, free = tr_item(kind, n, "laid")
                V.tensor_copy(rsb[:, :], bank[:, 0:T]).then_inc(free, 1)
                ve.wait_ge(*tr_done(kind, n, "laid"))
                settle()

            def pre(n):
                mean("pre", n)
                for k in range(KD):
                    V.scalar_tensor_tensor(hT[:, k, :], xT[:, k, :], gs[:, n, k:k + 1], rsb[:, :],
                                           ALU.mult, ALU.mult).then_inc(hx_ready, 1)

            def post(n):
                mean("post", n)
                for k in range(KD):
                    src = yacc[:, k, :] if n == 3 else Yk[:, k, :]
                    V.scalar_tensor_tensor(scr[:, k, :], src, gg[:, n, k:k + 1], rsb[:, :],
                                           ALU.mult, ALU.mult).then_inc(upd_ready, 1)

            def ada(n, g):
                bank, free = tr_item("adat", n, g)
                cols = bank[:, 0:2 * P].rearrange("p (j c x) -> p j c x", j=2, c=4)[:, :, :, 0]
                m = slice(g * KD, (g + 1) * KD)
                V.tensor_tensor(mod[:, n, m].rearrange("p (c j) -> p j c", j=2), cols,
                                bada[:, n, m].rearrange("p (c j) -> p j c", j=2), ALU.add).then_inc(free, 1)
                l, s = n // 2, 2 * (n % 2)
                if g:
                    ve.wait_ge(*tr_done("adat", n, g))
                if g == 1:
                    mark(V.scalar_tensor_tensor(gs[:, n, :], mod[:, n, m], 1.0, gn[:, l, s, :], ALU.add, ALU.mult))
                if g == 2:
                    mark(V.tensor_tensor(gg[:, n, :], mod[:, n, m], gn[:, l, s + 1, :], ALU.mult))

            def mixer(l):
                def pj_item(name):
                    ve.wait_ge(pj_full, PJ.full((name, l)))
                    return pj[PJ.bank((name, l))], pj_free[PJ.bank((name, l))]

                def negmaxes(kind, *units):
                    for u in units:
                        name = ((kind, u), l)
                        i, keys = (u if kind == "a" else 8 + u), (u % 2 + 1) * P
                        ve.wait_ge(sc_full, SC.full(name))
                        bank = sc[SC.bank(name)].rearrange("p (a t) -> p a t", a=2)
                        V.tensor_reduce(nm[:, i, :], bank[:, :, 0:keys], AX.X, ALU.max, negate=True).then_inc(negmax, 1)

                def combine(h):
                    for b in range(TB):
                        ve.wait_ge(*sc_done("a", 2 * h + b, l))
                    if h >= 2:
                        ve.wait_ge(tr_full, TR.full((f"at{h - 2}", l)))
                    r = rc[:, 2 * h:2 * h + 2, :]
                    mark(V.reciprocal(r, se[:, 2 * h:2 * h + 2, :]))
                    settle()
                    mark(V.tensor_tensor(r, r, lam_v[:, l:l + 1, :].to_broadcast([P, 2, 2]), ALU.mult))
                    settle()
                    for b in range(TB):
                        u, n = 2 * h + b, (b + 1) * P
                        e2 = E[:, u % 4, T:T + n]
                        mark(V.tensor_scalar(e2, e2, rc[:, u, 1:2], None, ALU.mult))
                    settle()
                    for b in range(TB):
                        u, n = 2 * h + b, (b + 1) * P
                        last = V.scalar_tensor_tensor(aA[:, h % 2, b * P:b * P + n], E[:, u % 4, 0:n], rc[:, u, 0:1],
                                                      E[:, u % 4, T:T + n], ALU.mult, ALU.add)
                    last.then_inc(combined, 1)

                mark(V.memset(raw[:, :, 0:CW - 1], 0.0))
                mark(V.memset(vbx[:, :, :, BD:BD + 1].rearrange("p b h o -> p (b h) o"), 1.0))
                mark(V.memset(scr[:, 7, :], 0.0))
                for b in range(TB):
                    ve.wait_ge(*pj_done(f"lat{b}", l))
                V.tensor_scalar(ms[:, MS[("c", l)], 0:4], ss[:, :], EPS, None, ALU.add).then_inc(mean_ready, 1)
                bank, free = pj_item("a1")
                V.tensor_copy(qkA[:, 2:4, :], bank.rearrange("p (a t) -> p a t", a=2)).then_inc(free, 1)
                bank, free = pj_item("va")
                V.tensor_copy(va, bank.rearrange("p (a t) -> p a t", a=2)).then_inc(free, 1)
                r = root(("c", l))
                for b in range(TB):
                    V.tensor_scalar(latn[:, b, 0:P], lat[:, b, 12:12 + P], r[:, b:b + 1], None, ALU.mult)
                    V.tensor_scalar(latn[:, b, 256:320], lat[:, b, 12 + P:12 + CQL], r[:, b:b + 1], None, ALU.mult)
                    last = V.tensor_scalar(latn[:, b, P:2 * P], lat[:, b, 12 + CQL:12 + CQL + CKV], r[:, 2 + b:3 + b],
                                           None, ALU.mult)
                last.then_inc(latn_ready, 1)
                bank, free = tr_item("lx", l)
                V.tensor_scalar(cqT, bank[:, 0:T], gq[:, l, 0:1], None, ALU.mult)
                V.tensor_scalar(ckT, bank[:, T:2 * T], gkv[:, l:l + 1], None, ALU.mult).then_inc(free, 1)
                bank, free = tr_item("lz", l)
                V.tensor_scalar(zT[0:64, :], bank[0:64, 0:T], gq[0:64, l, 1:2], None, ALU.mult)
                V.tensor_copy(zT[64:96, :], bank[64:96, 0:T])
                V.tensor_scalar(g_i[0:BH, :], bank[0:BH, T:2 * T], bg[:, l, 0:1], None, ALU.add).then_inc(free, 1)
                bank, free = tr_item("lf", l)
                V.tensor_scalar(g_f[0:BH, :], bank[0:BH, 0:T], bg[:, l, 1:2], None, ALU.add).then_inc(free, 1)
                ve.wait_ge(*tr_done("lf", l))
                V.scalar_tensor_tensor(g_n[0:BH, :], g_f[0:BH, :], -1.0, g_f[0:BH, :], ALU.mult,
                                       ALU.min).then_inc(gate_in, 1)
                negmaxes("a", 0, 1)
                for p in range(3):
                    bank, free = pj_item(f"uk{p}")
                    V.tensor_copy(kall[0:CN, 2 * p:2 * p + 2, :],
                                  bank[0:CN, :].rearrange("p (a t) -> p a t", a=2)).then_inc(free, 1)
                for b in range(TB):
                    bank, free = pj_item(f"uv{b}")
                    V.tensor_copy(vc[:, b, :], bank[:, 0:CH * CV]).then_inc(free, 1)
                negmaxes("a", 2, 3)
                ve.wait_ge(gate_ln, l + 1)
                G = slice(0, BH)
                zero = scr[G, 7, :]
                mark(V.scalar_tensor_tensor(g_f[G, :], g_f[G, :], 0.0, g_e[G, :], ALU.min, ALU.subtract))
                settle()
                mark(V.tensor_tensor_scan(g_b[G, :], g_f[G, :], zero, 0.0, ALU.add, ALU.add))
                settle()
                mark(V.tensor_tensor(g_a[G, :], g_i[G, :], g_b[G, :], ALU.subtract))
                settle()
                mark(V.tensor_tensor_scan(g_m[G, :], g_a[G, :], zero, 0.0, ALU.max, ALU.max))
                settle()
                mark(V.scalar_tensor_tensor(g_b[G, :], g_b[G, :], -1.0, g_m[G, :], ALU.mult, ALU.subtract))
                settle()
                V.tensor_scalar(g_m[G, :], g_m[G, :], -1.0, None, ALU.mult).then_inc(gates_ready, 1)
                negmaxes("a", 4, 5, 6, 7)
                combine(0)
                combine(1)
                ve.wait_ge(qcos_ready, 2 * (l + 1))
                R = slice(CN, CN + CR)
                for i in range(4):
                    name = (("rot", i), l)
                    ve.wait_ge(sc_full, SC.full(name))
                    nh = 2 if i < 3 else 1
                    bank = sc[SC.bank(name)][R, 0:nh * T].rearrange("p (a t) -> p a t", a=nh)
                    mark(V.tensor_tensor(bank, bank, sin[R, :].rearrange("p (o t) -> p o t", o=1).to_broadcast([CR, nh, T]),
                                         ALU.mult))
                    settle()
                    dst = qall[R, 2 * i:2 * i + 2, :] if i < 3 else kro[R, :].rearrange("p (o t) -> p o t", o=1)
                    V.tensor_tensor(dst, bank, qcos[R, 2 * i:2 * i + nh, :], ALU.add).then_inc(sc_free[SC.bank(name)], 1)
                for i in range(3):
                    ve.wait_ge(*pj_done(f"qk{i}", l))
                settle()
                for i in range(6):
                    mark(V.tensor_scalar(cv[:, i, :], raw[:, i, CW - 1:CW - 1 + T], wc[:, l, CW - 1, i:i + 1],
                                         bc[:, l, i:i + 1], ALU.mult, ALU.add))
                for j in range(CW - 2, -1, -1):
                    settle()
                    for i in range(6):
                        last = V.scalar_tensor_tensor(cv[:, i, :], raw[:, i, j:j + T], wc[:, l, j, i:i + 1], cv[:, i, :],
                                                      ALU.mult, ALU.add)
                        if j or i < 5:
                            mark(last)
                last.then_inc(conv_ready, 1)
                combine(2)
                combine(3)
                negmaxes("c", 0, 1, 2, 3)
                for b in range(TB):
                    bank, free = pj_item(f"vb{b}")
                    V.tensor_copy(vbx[:, b, :, 0:BD], bank[:, 0:BH * BD].rearrange("p (h d) -> p h d", h=BH)).then_inc(free, 1)
                ve.wait_ge(ao_sq, l + 1)
                mark(V.tensor_reduce(red[:, 0:8], sqj[:, 0:8 * AV].rearrange("p (a d) -> p a d", d=AV), AX.X, ALU.add))
                settle()
                V.tensor_scalar(ms[:, MS[("a", l)], 0:8], red[:, 0:8], 1.0 / AV, EPS, ALU.mult, ALU.add).then_inc(mean_ready, 1)
                negmaxes("c", 4)
                r = root(("a", l))[:, 0:8].rearrange("p (b h o) -> p b h o", b=TB, o=1).to_broadcast([P, TB, AH, AV])
                bank, free = tr_item("ao", l)
                V.tensor_tensor(tok[:, :, 0:AH * AV].rearrange("p b (h d) -> p b h d", h=AH),
                                bank.rearrange("p (b h d) -> p b h d", b=TB, h=AH), r, ALU.mult).then_inc(free, 1)

                def pt(u):
                    p, b = u // 2, u % 2
                    bank, free = tr_item(f"pt{u}", l)
                    o, n = 2 * b * P, 2 * (b + 1) * P
                    V.tensor_copy(PT[:, p, o:o + n], bank[:, 0:n]).then_inc(free, 1)

                pt(1)
                negmaxes("c", 5)
                pt(3)
                pt(5)
                mark(V.reciprocal(rc[:, 8:14, :], se[:, 8:14, :]))
                for h in range(BH):
                    name = (("s", h), l)
                    ve.wait_ge(sc_full, SC.full(name))
                    ve.wait_ge(*sc_done("w", h, l))
                    V.scalar_tensor_tensor(scw[:, h, :], sc[SC.bank(name)][:, 0:3 * P], SC_B, W[:, h % 2, :],
                                           ALU.mult, ALU.mult).then_inc(sc_free[SC.bank(name)], 1)
                settle()
                for b in range(TB):
                    bank, free = tr_item(f"co{b}", l)
                    r = rc[:, 8:14, :].rearrange("p (q b) j -> p b q j", b=TB)[:, b, :, :]
                    r = r.rearrange("p q (j o) -> p q j o", o=1).to_broadcast([P, 3, 2, CV])
                    o = tok[:, b, D - CH * CV:D].rearrange("p (q j d) -> p q j d", q=3, j=2)
                    V.tensor_tensor(o, bank[:, 0:CH * CV].rearrange("p (q j d) -> p q j d", q=3, j=2), r,
                                    ALU.mult).then_inc(free, 1)
                bo = []
                for b in range(TB):
                    bank, free = tr_item(f"bo{b}", l)
                    bank = bank[:, 0:BH * (BD + 1)].rearrange("p (h d) -> p h d", h=BH)
                    bo.append((bank, free))
                    mark(V.tensor_copy(den[:, b * BH:(b + 1) * BH].rearrange("p (h o) -> p h o", o=1),
                                       bank[:, :, BD:BD + 1]))
                settle()
                ve.wait_ge(*tr_done("gt", l))
                mark(V.scalar_tensor_tensor(rden[:, :], den[:, :], -1.0, den[:, :], ALU.mult, ALU.max))
                settle()
                mark(V.tensor_tensor(den[:, :], rden[:, :], em[:, :], ALU.max))
                settle()
                mark(V.reciprocal(rden[:, :], den[:, :]))
                settle()
                for b, (bank, free) in enumerate(bo):
                    r = rden[:, b * BH:(b + 1) * BH].rearrange("p (h o) -> p h o", o=1).to_broadcast([P, BH, BD])
                    V.tensor_tensor(hb[:, b * BH:(b + 1) * BH, :], bank[:, :, 0:BD], r, ALU.mult).then_inc(free, 1)
                ve.wait_ge(hb_sq, l + 1)
                mark(V.tensor_reduce(red[:, :], sqj[:, :].rearrange("p (a d) -> p a d", d=BD), AX.X, ALU.add))
                settle()
                V.tensor_scalar(ms[:, MS[("b", l)], 0:12], red[:, :], 1.0 / BD, EPS, ALU.mult, ALU.add).then_inc(mean_ready, 1)
                r = root(("b", l)).rearrange("p (b h o) -> p b h o", b=TB, o=1).to_broadcast([P, TB, BH, BD])
                V.tensor_tensor(tok[:, :, AH * AV:AH * AV + BH * BD].rearrange("p b (h d) -> p b h d", h=BH),
                                hb.rearrange("p (b h) d -> p b h d", b=TB), r, ALU.mult).then_inc(tok_ready, 1)
                for n, g in ADA_MIXER[l]:
                    ada(n, g)
                ve.wait_ge(obt_ready, l + 1)
                bank, free = tr_item("mt1", l)
                for j in range(2):
                    last = V.scalar_tensor_tensor(mixT[:, 2 + j, :], bank[:, j * T:(j + 1) * T], gml[:, l, j:j + 1],
                                                  obt[:, j, :], ALU.mult, ALU.mult)
                last.then_inc(free, 1)
                bank, free = tr_item("mt2", l)
                V.scalar_tensor_tensor(mixT[:, 4, :], bank[:, 0:T], gml[:, l, 2:3], obt[:, 2, :], ALU.mult, ALU.mult)
                V.tensor_copy(mixT[:, 5, :], bank[:, T:2 * T]).then_inc(free, 1)

            ve.wait_ge(param_in, 16 * n_param)
            for i in range(2):
                V.tensor_tensor(lam_pr[:, i, :], lam_in[:, i, :], lam_in[:, 2 + i, :], ALU.mult).then_inc(lam_prod, 1)
            bank, free = tr_item("param1")
            V.tensor_copy(pcol[:, 0, 0:124], bank[:, 0:124]).then_inc(free, 1)
            bank, free = tr_item("param2")
            V.tensor_copy(pcol[:, 1, 0:112], bank[:, 0:112]).then_inc(free, 1)
            for l in range(L):
                mark(V.tensor_scalar(gd[:, l:l + 1], gdr[:, l:l + 1], 1.0 - LAM0[l], None, ALU.mult))
                mark(V.memset(lam_v[:, l, 0:1], 1.0))
            R = slice(CN, CN + CR)
            ang, k_f, k_i = E[R, 0, 0:T], E[R, 1, 0:T], E[R, 2, 0:T].bitcast(I32)
            s_, c_, w_ = sin[R, :], cos[R, :], E[R, 3, 0:T]
            mark(V.tensor_copy(ang, posi[R, :]))
            settle()
            mark(V.tensor_scalar(ang, ang, con[R, C_FREQ:C_FREQ + 1], None, ALU.mult))
            settle()
            mark(V.tensor_scalar(k_i, ang, 1.0 / TWO_PI, None, ALU.mult))
            settle()
            mark(V.tensor_copy(k_f, k_i))
            settle()
            for part in (PI_1, PI_2, PI_3):
                mark(V.scalar_tensor_tensor(ang, k_f, -part, ang, ALU.mult, ALU.add))
                settle()

            def wrap(x):
                mark(V.tensor_scalar(w_, x, PI_LOW, -TWO_PI, ALU.is_gt, ALU.mult))
                settle()
                mark(V.tensor_tensor(x, x, w_, ALU.add))
                settle()

            wrap(ang)
            mark(V.tensor_scalar(c_, ang, np.pi / 2, None, ALU.add))
            settle()
            wrap(c_)
            V.tensor_scalar(s_, ang, -PI_LOW, PI_LOW, ALU.max, ALU.min).then_inc(rope_in, 1)
            V.tensor_scalar(c_, c_, -PI_LOW, PI_LOW, ALU.max, ALU.min).then_inc(rope_in, 1)
            ve.wait_ge(*tr_done("lam"))
            for l in range(L):
                mark(V.tensor_tensor(lam_v[:, l, 1:2], lam_e[:, 1, l:l + 1], lam_e[:, 0, l:l + 1], ALU.subtract))
            settle()
            for l in range(L):
                mark(V.tensor_scalar(lam_v[:, l, 1:2], lam_v[:, l, 1:2], -LAM0[l], None, ALU.add))
            ve.wait_ge(*tr_done("param2"))
            for n, g in ADA_START:
                ada(n, g)
            ve.wait_ge(y_quarter, 4)
            pre(0)
            mixer(0)
            post(0)
            ve.wait_ge(x_upd, KD)
            pre(1)
            for t in range(FT):
                ve.wait_ge(silu_done, t + 1)
                if t >= 2:
                    ve.wait_ge(down_done, t - 1)
                V.tensor_tensor(act[:, t % 2, :], PG[:, t % 2, T:2 * T], sg[:, t % 2, :], ALU.mult).then_inc(act_ready, 1)
                if t % 4 == 3:
                    ada(*ADA_DENSE[t // 4])
            post(1)
            ve.wait_ge(x_upd, 2 * KD)
            pre(2)
            mixer(1)
            post(2)
            ve.wait_ge(x_upd, 3 * KD)
            pre(3)

            bank, free = tr_item("router")
            V.tensor_tensor(lg, bank[:, 0:TB * NE].rearrange("p (b e) -> p b e", b=TB),
                            rbias[:, :].rearrange("p (o e) -> p o e", o=1).to_broadcast([P, TB, NE]), ALU.add).then_inc(free, 1)
            ve.wait_ge(*tr_done("router"))
            for b in range(TB):
                mark(V.max(mx8[:, b, :], lg[:, b, :]))
            settle()
            for b in range(TB):
                mark(V.max_index(ix8[:, b, :], mx8[:, b, :], lg[:, b, :]))
            V.tensor_tensor(gt2[:, :, 0:1], mx8[:, :, 1:2], mx8[:, :, 0:1], ALU.subtract).then_inc(gap_ready, 1)
            settle()
            mark(V.tensor_copy(ixf, ix8[:, :, :]))
            ve.wait_ge(gap_exp, 1)
            mark(V.tensor_scalar(gt2[:, :, 2:3], gt2[:, :, 1:2], 1.0, None, ALU.add))
            settle()
            mark(V.reciprocal(gt2[:, :, 0:1], gt2[:, :, 2:3]))
            settle()
            mark(V.tensor_tensor(gt2[:, :, 3:4], gt2[:, :, 1:2], gt2[:, :, 0:1], ALU.mult))
            settle()
            for b in range(TB):
                mark(V.tensor_scalar(oh1[:, b, :], iota[:, 0:NE], ixf[:, b, 0:1], None, ALU.is_equal))
                mark(V.tensor_scalar(oh2[:, b, :], iota[:, 0:NE], ixf[:, b, 1:2], None, ALU.is_equal))
            settle()
            for b in range(TB):
                mark(V.tensor_scalar(Gm[:, b, :], oh1[:, b, :], gt2[:, b, 0:1], None, ALU.mult))
            settle()
            for b in range(TB):
                mark(V.scalar_tensor_tensor(Gm[:, b, :], oh2[:, b, :], gt2[:, b, 3:4], Gm[:, b, :], ALU.mult, ALU.add))
            V.tensor_tensor(Mm, oh1, oh2, ALU.add).then_inc(routed, 1)
            bank, free = tr_item("rank")
            V.tensor_copy(pos, bank[:, 0:TB * NE].rearrange("p (b e) -> p b e", b=TB))
            V.tensor_copy(cnt[:, :], bank[:, 2 * NE:3 * NE]).then_inc(free, 1)
            ve.wait_ge(*tr_done("rank"))
            settle()
            ve.wait_ge(routed, 1)
            ve.wait_ge(yacc_zero, 2)

            with ve.Fori(0, NE) as e:
                n_tok = ve.value_load(cnt[0:1, bass.ds(e, 1)], min_val=0, max_val=T)
                for b in range(TB):
                    V.tensor_scalar(oh[:, b, :], iota, pos[:, b, bass.ds(e, 1)], Mm[:, b, bass.ds(e, 1)],
                                    ALU.is_equal, ALU.mult)
                    last = V.tensor_scalar(ohg[:, b, :], iota, pos[:, b, bass.ds(e, 1)], Gm[:, b, bass.ds(e, 1)],
                                           ALU.is_equal, ALU.mult)
                last.then_inc(hot_ready, 1)

                def copy(o, i_):
                    return V.tensor_copy(o, i_)

                def expert(n):
                    def item(i):
                        ve.wait_ge(ax_full, e * AX_T + (i + 1))
                        return tr[i % 2]

                    for i in (1, 3):
                        bank = item(i)
                        V.tensor_copy(mixT[:, 2 * i:2 * i + 2, 0:n],
                                      bank.rearrange("p (a t) -> p a t", a=2)[:, :, 0:n]).then_inc(ax_free[1], 1)
                    bank = item(5)
                    for j, m in blocks(n):
                        last = V.tensor_copy(gPT[0:m, j, P:2 * P], bank[0:m, j * P:(j + 1) * P])
                    last.then_inc(ax_free[1], 1)
                    for t in range(FT):
                        ve.wait_ge(silu_done, e * FT + (FT + t + 1))
                        ve.wait_ge(down_done, e * FT + (FT + t - 1))
                        V.tensor_tensor(act[:, t % 2, 0:n], PG[:, t % 2, T:T + n], sg[:, t % 2, 0:n],
                                        ALU.mult).then_inc(act_ready, 1)
                    ve.wait_ge(down_done, e * FT + 2 * FT)
                    ye_half(copy, n, 1)
                    for i in (7, 9):
                        bank = item(i)
                        for j, m in blocks(n):
                            c = 2 * (i - 6) * P
                            last = V.tensor_copy(yeK[0:m, j, c:c + T], bank[0:m, j * T:(j + 1) * T])
                        last.then_inc(ax_free[1], 1)
                    for i in range(10, 14):
                        bank = item(i)
                        o = yacc[:, 2 * (i - 10):2 * (i - 10) + 2, :]
                        V.tensor_tensor(o, o, bank.rearrange("p (a t) -> p a t", a=2), ALU.add).then_inc(ax_free[i % 2], 1)

                variants(ve, n_tok, expert)
            for b in range(2):
                ve.wait_ge(ax_free[b], (NE + 1) * AX_F)
            ve.sem_inc(yacc_ready, 4 * NE)
            post(3)

        @block.gpsimd
        def _(po):
            G = nc.gpsimd

            def roots(name, n):
                G.tensor_tensor(rs[:, MS[name], 0:n], ms[:, MS[name], 0:n], half[:, 0:n], ALU.pow).then_inc(rstd_ready, 1)

            def norm_roots(kind, n):
                po.wait_ge(*tr_done(kind, n, "total"))
                G.tensor_tensor(root_[:, :], meps[:, :], half[:, 0:TB], ALU.pow).then_inc(rstd_ready, 1)

            def update(n):
                for k in range(KD):
                    po.wait_ge(upd_ready, KD * n + k + 1)
                    G.tensor_tensor(xT[:, k, :], xT[:, k, :], scr[:, k, :], ALU.add).then_inc(x_upd, 1)

            def mixer(l):
                for b in range(TB):
                    po.wait_ge(*pj_done(f"lat{b}", l))
                G.tensor_copy(latn[:, :, 320:352], lat[:, :, LATW - CR:LATW]).then_inc(kr_ready, 1)
                po.wait_ge(mean_ready, 3 * l + 1)
                po.wait_ge(kr_ready, l + 1)
                roots(("c", l), 4)
                R = slice(CN, CN + CR)
                cs = cos[R, :].rearrange("p (o t) -> p o t", o=1)
                po.wait_ge(*pj_done("uq1", l))
                po.wait_ge(*pj_done("uq2", l))
                po.wait_ge(rope_set, 2)
                po.wait_ge(rstd_ready, RS[("c", l)] + 1)
                G.tensor_tensor(qcos[R, 0:CH, :], qall[R, :, :], cs.to_broadcast([CR, CH, T]), ALU.mult).then_inc(qcos_ready, 1)
                G.tensor_tensor(qcos[R, CH, :], zT[R, :], cos[R, :], ALU.mult).then_inc(qcos_ready, 1)
                po.wait_ge(*sc_done("rot", 3, l))
                po.wait_ge(qcos_ready, 2 * (l + 1))
                G.tensor_copy(kall[R, :, :], kro[R, :].rearrange("p (o t) -> p o t", o=1).to_broadcast([CR, CH, T])).then_inc(rope_done, 1)
                po.wait_ge(obt_tanh, l + 1)
                po.wait_ge(rope_done, l + 1)
                G.tensor_scalar(obt, obt, 1.0, 0.5, ALU.add, ALU.mult).then_inc(obt_ready, 1)
                po.wait_ge(mean_ready, 3 * l + 2)
                roots(("a", l), 8)
                po.wait_ge(mean_ready, 3 * l + 3)
                roots(("b", l), 12)

            G.memset(ones[:, :], 1.0).then_inc(const_set, 1)
            G.memset(half[:, :], -0.5).then_inc(const_set, 1)
            G.memset(ccol[:, :, :], 0.0).then_inc(const_set, 1)
            po.wait_ge(const_set, 3)
            for l in range(L):
                norm_roots("pre", 2 * l)
                mixer(l)
                norm_roots("post", 2 * l)
                update(2 * l)
                norm_roots("pre", 2 * l + 1)
                if l == 1:
                    G.memset(yacc, 0.0).then_inc(yacc_zero, 1)
                    G.memset(yeT, 0.0).then_inc(yacc_zero, 1)
                norm_roots("post", 2 * l + 1)
                update(2 * l + 1)


_INS = ["x", "c", "positions", "w_ada", "b_ada", "g_norm", "w_in", "w_out", "lam_q1", "lam_k1", "lam_q2", "lam_k2",
        "g_diff", "w_conv", "b_conv", "b_igate", "b_fgate", "g_mlstm", "g_q_lat", "g_kv_lat", "w_uq", "w_ukv",
        "w_gate_d", "w_up_d", "w_down_d", "w_router", "b_router", "w_gate_e", "w_up_e", "w_down_e"]


def kernel(**inputs):
    import concourse.bacc as _bacc
    from concourse.bass_utils import run_bass_kernel_spmd as _run

    nc = _bacc.Bacc("TRN2", target_bir_lowering=False, num_devices=1)
    arrays, aps = {}, {}
    for name in _INS + ["consts"]:
        a = const_table() if name == "consts" else np.ascontiguousarray(inputs[name])
        arrays[f"in_{name}"] = a
        aps[name] = nc.dram_tensor(f"in_{name}", a.shape, mybir.dt.from_np(a.dtype), kind="ExternalInput").ap()
    result = nc.dram_tensor("result", (1, T, D), F32, kind="ExternalOutput").ap()
    build(nc, aps, result)
    r = _run(nc, [arrays], core_ids=[0])
    return r.results[0]["result"]
```

```python
from contextlib import ExitStack

import numpy as np

import concourse.bass as bass
from concourse import mybir

F32 = mybir.dt.float32
I32 = mybir.dt.int32
U32 = mybir.dt.uint32
ALU = mybir.AluOpType
ACT = mybir.ActivationFunctionType
AX = mybir.AxisListType

P = 128
T, D, L = 256, 1024, 2
TB = T // P
KD = D // P
CHUNK, EPS = 64, 1e-6
AH, AQ, AV = 4, 32, 64
BH, BD, CW = 6, 64, 4
CH, CQL, CKV, CN, CR, CV = 6, 192, 128, 64, 32, 64
FF, NE = 3584, 8
NEG = -1.0e30
COL_Q, COL_VA, COL_QK, COL_VB, COL_OB, COL_LAT = 0, 512, 768, 1536, 1920, 2304
IN_W = 2668
LATW = IN_W - COL_LAT
LAM0 = [0.8 - 0.6 * float(np.exp(-0.3 * l)) for l in range(L)]
SC_A, SC_B, SC_C = AQ ** -0.5, BD ** -0.5, (CN + CR) ** -0.5

ARENA = 24096
SLOTS, SW = 7, 256
FT = FF // P
STAGES = FT // 2
EARLY = SLOTS - D // SW
USES = 3 * STAGES
NVAR = (32, 64, 128, 160, 192, 256)
SLOTS_E = 2 * SLOTS

C_ID, C_TRI, C_CAUS, C_MU, C_MK, C_IOTA, C_ROT, C_FREQ, C_END = 0, 128, 256, 384, 512, 640, 896, 928, 929
TWO_PI = 2.0 * np.pi
PI_1 = 6.28125
PI_2 = float(np.float32(np.floor((TWO_PI - PI_1) * 2 ** 22) / 2 ** 22))
PI_3 = float(np.float32(TWO_PI - PI_1 - PI_2))
PI_LOW = 3.1415925


def const_table():
    t = np.zeros((P, C_END), np.float32)
    i = np.arange(P)
    t[:, C_ID:C_ID + P] = np.eye(P)
    t[:, C_TRI:C_TRI + P] = i[:, None] < i[None, :]
    t[:, C_CAUS:C_CAUS + P] = np.where(i[:, None] <= i[None, :], 0.0, NEG)
    t[:, C_MU:C_MU + P] = i[None, :] < CHUNK
    t[:, C_MK:C_MK + P] = np.where(i[None, :] < CHUNK, 0.0, NEG)
    t[:, C_IOTA:C_IOTA + T] = np.arange(T)
    for m in range(CR // 2):
        t[CN + CR // 2 + m, C_ROT + m] = -1.0
        t[CN + m, C_ROT + CR // 2 + m] = 1.0
    f = (10000.0 ** (-np.arange(0, CR, 2) / CR)).astype(np.float32)
    t[CN:CN + CR, C_FREQ] = np.concatenate([f, f])
    return t


def weight_uses():
    uses = []

    def ada(*thirds):
        uses.extend(("ada", n, 4 * g + c) for x in thirds if x for n, g in [x] for c in range(4))

    def w_in(l, a, b):
        uses.extend(("in", l, key) for key in W_IN_ORDER[a:b])

    def mixer(l):
        w_in(l, 0, 5)
        ada(ADA_MIXER[l][0])
        w_in(l, 5, 8)
        ada(ADA_MIXER[l][1])
        w_in(l, 8, 12)
        ada(*ADA_MIXER[l][2:4])
        uses.extend(("out", l, c) for c in range(D // SW))

    ada(*ADA_START)
    mixer(0)
    ada(ADA_NORM[1])
    for s in range(STAGES):
        uses.extend([("gate", 0, s), ("up", 0, s)])
        if s == 1:
            ada(ADA_DENSE)
        uses.append(("down", 0, s))
    ada(ADA_NORM[2])
    mixer(1)
    ada(ADA_NORM[3])
    return uses


def expert_uses():
    uses = []
    for s in range(STAGES):
        uses += [("gate", s), ("up", s)]
        if s:
            uses.append(("down", s - 1))
    return uses + [("down", STAGES - 1)]


W_IN_ORDER = [(COL_LAT, 256), (COL_LAT + 256, LATW - 256), (COL_Q, 256), (COL_Q + 256, 256), (COL_VA, 256),
              (COL_QK, 256), (COL_QK + 256, 256), (COL_QK + 512, 256), (COL_OB, 256), (COL_OB + 256, 128),
              (COL_VB, 256), (COL_VB + 256, 128)]
ADA_START = [(0, 0), (0, 1)]
ADA_MIXER = [[(0, 2), (1, 0), (1, 1), (1, 2)], [None, (3, 0), (3, 1), (3, 2)]]
ADA_NORM = [None, (2, 0), (2, 2), None]
ADA_DENSE = (2, 1)
ADA_ORDER = ADA_START + ADA_MIXER[0] + [ADA_NORM[1], ADA_DENSE, ADA_NORM[2]] + ADA_MIXER[1] + [ADA_NORM[3]]
ROW_SLOT = {x: i % 2 for i, x in enumerate(x for x in ADA_ORDER if x)}
assert len(ROW_SLOT) == 2 * L * 3
IN_ITEM = dict(zip(W_IN_ORDER, ["lat1", "lat1", "a0", "a1", "va", "qk0", "qk1", "qk2", "ob0", "ob1", "vb1", "vb1"]))
PJ_LAYER = ["lat0", "lat1", "a0", "a1", "va", "qk0", "uq0", "uq1", "uq2", "uk0", "uk1", "uk2", "uv0", "uv1",
            "qk1", "qk2", "ob0", "ob1", "vb0", "vb1"]
SC_LAYER = ([("a", u) for u in range(8)] + [("rot", i) for i in range(4)] + [("c", u) for u in range(6)]
            + [(k, h) for h in range(BH) for k in ("w", "s")])
TR_LAYER = ["rows0", "lx", "lz", "lf", "cols0", "rows1", "at0", "at1", "cols1", "at2", "at3", "ao",
            *[f"pt{u}" for u in range(6)], "rows2", "gt", "cols2", "co0", "co1", "bo0", "bo1", "rows3",
            "mt0", "mt1", "mt2", "mt3", "cols3"]


class Ring:

    def __init__(self, names, n):
        self.at = {name: i for i, name in enumerate(names)}
        assert len(self.at) == len(names)
        self.n = n

    def bank(self, name):
        return self.at[name] % self.n

    def full(self, name):
        return self.at[name] + 1

    def before(self, name):
        return self.at[name] // self.n


def tr_names():
    def rows(x):
        return [("ada", *x)] if x else []

    def cols(x):
        return [("adat", *x)] if x else []

    def norm(kind, n):
        return [(kind, n, step) for step in ("partial", "total", "laid")]

    def pre(n):
        return rows(ADA_NORM[n]) + norm("pre", n) + cols(ADA_NORM[n])

    a, b = ADA_START
    names = pre(0) + ["param1", "param2", "lam"] + rows(a) + rows(b) + cols(a) + cols(b)
    for l in range(L):
        names += pre(2 * l) if l else []
        for x in TR_LAYER:
            if x[:4] in ("rows", "cols"):
                names += (rows if x[:4] == "rows" else cols)(ADA_MIXER[l][int(x[4])])
            else:
                names.append((x, l))
        names += norm("post", 2 * l) + pre(2 * l + 1)
        if l == 0:
            names += rows(ADA_DENSE) + cols(ADA_DENSE) + norm("post", 1)
    names += ["router", "rank"] + norm("post", 3)
    return names


def rs_names():
    names = []
    for l in range(L):
        names += [("pre", 2 * l), ("c", l), ("a", l), ("b", l), ("post", 2 * l), ("pre", 2 * l + 1), ("post", 2 * l + 1)]
    return names


def build(nc, ap, out):
    uses = weight_uses()
    n_before = len(uses)
    slot_of = [u % SLOTS for u in range(n_before)]
    expert_list = expert_uses()
    expert_at = {u: i for i, u in enumerate(expert_list)}
    assert len(expert_list) == USES and USES % SLOTS_E == 0
    use_at = {u: i for i, u in enumerate(uses)}
    PJ = Ring([(x, l) for l in range(L) for x in PJ_LAYER], 2)
    SC = Ring([(x, l) for l in range(L) for x in SC_LAYER], 4)
    TR = Ring(tr_names(), 2)
    MS = {name: i for i, name in enumerate([(kind, l) for l in range(L) for kind in "cab"])}
    RS = {name: i for i, name in enumerate(rs_names())}

    with ExitStack() as ctx:
        def sb(name, shape, dt=F32):
            return ctx.enter_context(nc.sbuf_tensor(name, shape, dt))

        def ps(name, shape):
            return ctx.enter_context(nc.psum_tensor(name, shape, F32))

        def sem(name):
            return ctx.enter_context(nc.semaphore(name))

        Y = ps("Y", [P, 4, 512])
        PG = ps("PG", [P, 2, 512])
        TRB = ps("TRB", [P, 2, 512])
        pj = [Y[:, 0, :], Y[:, 1, :]]
        sc = [Y[:, 2, :], Y[:, 3, :], PG[:, 0, :], PG[:, 1, :]]
        tr = [TRB[:, 0, :], TRB[:, 1, :]]
        Yf = Y[:, :, :].rearrange("p b c -> p (b c)")
        Yk = Yf.rearrange("p (k t) -> p k t", k=KD)

        ring = sb("ring", [P, SLOTS, KD, SW])
        xT = sb("xT", [P, KD, T])
        hT = sb("hT", [P, KD, T])
        scr = sb("scr", [P, KD, T])
        tok = sb("tok", [P, TB, D])
        mixT = sb("mixT", [P, KD, T])
        con = sb("con", [P, C_END])
        ones = sb("ones", [P, P])
        pcol = sb("pcol", [P, 2, P])
        ccol = sb("ccol", [P, KD, 32])
        s4 = sb("s4", [P, T])
        arow = sb("arow", [P, 2, SW])
        prow = arow[:, :, 0:P]
        meps = sb("meps", [P, TB])
        root_ = sb("root_", [P, TB])
        diag = sb("diag", [P, TB, P])
        mod = sb("mod", [P, 2 * L, 24])
        gs = sb("gs", [P, 2 * L, KD])
        gg = sb("gg", [P, 2 * L, KD])
        lam_in = sb("lam_in", [AQ, 4, L])
        lam_pr = sb("lam_pr", [AQ, 2, L])
        lam_e = sb("lam_e", [P, 2, L])
        lam_v = sb("lam_v", [P, L, 2])
        gq = sb("gq", [P, L, 2])
        gdr = sb("gdr", [P, L])
        gd = sb("gd", [P, L])
        bg = sb("bg", [BH, L, 2])
        rbias = sb("rbias", [P, NE])
        wr = sb("wr", [P, KD, NE])
        ms = sb("ms", [P, 3 * L, 12])
        rs = sb("rs", [P, 3 * L, 12])
        half = sb("half", [P, 12])
        rsb = sb("rsb", [P, T])
        cos = sb("cos", [P, T])
        sin = sb("sin", [P, T])
        posi = sb("posi", [P, T], I32)
        ss = sb("ss", [P, 4])
        red = sb("red", [P, 12])
        den = sb("den", [P, 12])
        rden = sb("rden", [P, 12])
        aK = sb("aK", [P, 12])
        em = sb("em", [P, 12])
        nm = sb("nm", [P, 14, 2])
        se = sb("se", [P, 14, 2])
        rc = sb("rc", [P, 14, 2])

        arena = sb("arena", [P, ARENA])
        cnt = sb("cnt", [P, NE], I32)
        ix8 = sb("ix8", [P, TB, NE], U32)
        top = {"mixer": 0, "ffn": 0}

        def cut(user, *dims):
            n = int(np.prod(dims))
            a = arena[:, top[user]:top[user] + n]
            top[user] += n
            return shaped(a, *dims)

        def shaped(a, *dims):
            if len(dims) == 2:
                a = a.rearrange("p (a b) -> p a b", a=dims[0])
            if len(dims) == 3:
                a = a.rearrange("p (a b c) -> p a b c", a=dims[0], b=dims[1])
            return a

        wuq = cut("mixer", 2, CH * (CN + CR))
        wukv = cut("mixer", CH * (CN + CV))
        qkA = cut("mixer", 4, T)
        va = cut("mixer", TB, AH * AV)
        lat_at = top["mixer"]
        lat = cut("mixer", TB, LATW)
        latn = cut("mixer", TB, 352)
        cqT = cut("mixer", T)
        ckT = cut("mixer", T)
        zT = cut("mixer", T)
        qall = cut("mixer", CH, T)
        kall = cut("mixer", CH, T)
        vc = cut("mixer", TB, CH * CV)
        E = cut("mixer", 4, 2 * T)
        aA = cut("mixer", 2, 3 * P)
        aT = cut("mixer", AH, 3 * P)
        conv_at = top["mixer"]
        raw = cut("mixer", 6, T + CW - 1)
        cv = cut("mixer", 6, T)
        PT = cut("mixer", CH // 2, 6 * P)
        vbx = cut("mixer", TB, BH, BD + 1)
        sqj = cut("mixer", 3 * T)
        g_i, g_f, g_n, g_e, g_a, g_m, g_b = (cut("mixer", T) for _ in range(7))
        obt = shaped(arena[:, lat_at:lat_at + 3 * T], 3, T)
        qcos = shaped(PT.rearrange("p a b -> p (a b)")[:, 0:(CH + 1) * T], CH + 1, T)
        scw = shaped(arena[:, conv_at:conv_at + BH * 3 * P], BH, 3 * P)
        W = shaped(arena[:, conv_at + BH * 3 * P:conv_at + (BH + 2) * 3 * P], 2, 3 * P)
        hb = shaped(E.rearrange("p a b -> p (a b)")[:, 0:TB * BH * BD], TB * BH, BD)
        scrf = scr[:, :, :].rearrange("p k t -> p (k t)")
        qks = scr[:, 0:6, :]
        kro = scr[:, 6, :]
        act = cut("ffn", 2, T)
        sg = cut("ffn", 2, T)
        yacc = cut("ffn", KD, T)
        sgK = cut("ffn", 2, SW)
        actK = cut("ffn", 2, SW)
        actT = cut("ffn", 2, 2, P)
        yeK = cut("ffn", TB, D)
        oh = cut("ffn", TB, T)
        ohg = cut("ffn", TB, T)
        gPT = cut("ffn", TB, T)
        lg = cut("ffn", TB, NE)
        mx8 = cut("ffn", TB, NE)
        ixf = cut("ffn", TB, NE)
        gt2 = cut("ffn", TB, 4)
        oh1 = cut("ffn", TB, NE)
        oh2 = cut("ffn", TB, NE)
        Gm = cut("ffn", TB, NE + 1)
        Mm = cut("ffn", TB, NE + 1)
        pos = cut("ffn", TB, NE + 1)
        ring_e = [ring[:, (n_before + i) % SLOTS, :, :] for i in range(SLOTS)] + [cut("ffn", KD, SW) for _ in range(SLOTS_E - SLOTS)]
        assert max(top.values()) <= ARENA, top

        ident = con[:, C_ID:C_ID + P]
        tri = con[:, C_TRI:C_TRI + P]
        caus = con[:, C_CAUS:C_CAUS + P]
        iota = con[:, C_IOTA:C_IOTA + T]

        gn = pcol[:, 0, 0:64].rearrange("p (l s k) -> p l s k", l=L, s=4)
        wc = pcol[:, 0, 64:112].rearrange("p (l j i) -> p l j i", l=L, j=CW)
        bc = pcol[:, 0, 112:124].rearrange("p (l i) -> p l i", l=L)
        bada = pcol[:, 1, 0:96].rearrange("p (n k) -> p n k", n=2 * L)
        craw = pcol[:, 1, 96:104]
        gml = pcol[:, 1, 104:110].rearrange("p (l i) -> p l i", l=L)
        gkv = pcol[:, 1, 110:112]

        rows1 = [(0, 64, ap["g_norm"].rearrange("l s (k p) -> (l s k) p", p=P)),
                 (64, 112, ap["w_conv"].rearrange("l j (k p) -> (l j k) p", p=P)),
                 (112, 124, ap["b_conv"].rearrange("l (k p) -> (l k) p", p=P))]
        rows2 = [(0, 96, ap["b_ada"].rearrange("l s (k p) -> (l s k) p", p=P)),
                 (96, 104, ap["c"].rearrange("b (k p) -> (b k) p", p=P)),
                 (104, 110, ap["g_mlstm"].rearrange("l (k p) -> (l k) p", p=P)),
                 (110, 112, ap["g_kv_lat"])]
        params = [(prow[a:b, i, :], src) for i, rows_ in enumerate((rows1, rows2)) for a, b, src in rows_]
        params += [(lam_in[:, i, :], ap[name].rearrange("l d -> d l"))
                   for i, name in enumerate(("lam_q1", "lam_q2", "lam_k1", "lam_k2"))]
        params += [(gdr[i * AV:(i + 1) * AV, :], ap["g_diff"].rearrange("l d -> d l")) for i in range(2)]
        params += [(gq[:, :, 0], ap["g_q_lat"][:, 0:P].rearrange("l d -> d l")),
                   (gq[0:CQL - P, :, 1], ap["g_q_lat"][:, P:CQL].rearrange("l d -> d l")),
                   (bg[:, :, 0], ap["b_igate"].rearrange("l h -> h l")),
                   (bg[:, :, 1], ap["b_fgate"].rearrange("l h -> h l")),
                   (rbias[:, :], ap["b_router"].to_broadcast([P, NE])),
                   (wr[:, :, :], ap["w_router"][0].rearrange("(k p) e -> p k e", p=P)),
                   (posi[CN:CN + CR, :], ap["positions"].to_broadcast([CR, T]))]
        n_param = len(params)

        param_in = sem("param_in")
        x_in = sem("x_in")
        wl_in = sem("wl_in")
        landed = [sem(f"landed{i}") for i in range(SLOTS)]
        landed_e = [sem(f"landed_e{i}") for i in range(SLOTS_E)]
        out_read = sem("out_read")
        const_set = sem("const_set")
        pj_full = sem("pj_full")
        pj_free = [sem(f"pj_free{i}") for i in range(2)]
        sc_full = sem("sc_full")
        sc_free = [sem(f"sc_free{i}") for i in range(4)]
        tr_full = sem("tr_full")
        tr_free = [sem(f"tr_free{i}") for i in range(2)]
        y_full = sem("y_full")
        diag_ready = sem("diag_ready")
        y_quarter = sem("y_quarter")
        sq_ready = sem("sq_ready")
        mean_ready = sem("mean_ready")
        rstd_ready = sem("rstd_ready")
        hx_ready = sem("hx_ready")
        h_ready = sem("h_ready")
        upd_ready = sem("upd_ready")
        x_upd = sem("x_upd")
        x_updv = sem("x_updv")
        ccol_ready = sem("ccol_ready")
        mod_ready = sem("mod_ready")
        lam_prod = sem("lam_prod")
        rope_in = sem("rope_in")
        rope_set = sem("rope_set")
        dve_seq = sem("dve_seq")
        act_seq = sem("act_seq")
        pool_seq = sem("pool_seq")
        latn_ready = sem("latn_ready")
        kr_ready = sem("kr_ready")
        gate_in = sem("gate_in")
        gate_exp = sem("gate_exp")
        gate_ln = sem("gate_ln")
        gates_ready = sem("gates_ready")
        conv_ready = sem("conv_ready")
        qks_ready = sem("qks_ready")
        obt_tanh = sem("obt_tanh")
        obt_ready = sem("obt_ready")
        qcos_ready = sem("qcos_ready")
        rope_done = sem("rope_done")
        negmax = sem("negmax")
        combined = sem("combined")
        ao_sq = sem("ao_sq")
        hb_sq = sem("hb_sq")
        tok_ready = sem("tok_ready")
        gu_full = sem("gu_full")
        silu_done = sem("silu_done")
        act_ready = sem("act_ready")
        down_done = sem("down_done")
        gap_ready = sem("gap_ready")
        gap_exp = sem("gap_exp")
        routed = sem("routed")
        htok_ready = sem("htok_ready")
        hot_ready = sem("hot_ready")
        ax_full = sem("ax_full")
        ax_free = [sem(f"ax_free{i}") for i in range(4)]
        tp_full = sem("tp_full")
        at_ready = sem("at_ready")
        ye_ready = sem("ye_ready")
        yacc_zero = sem("yacc_zero")
        yacc_ready = sem("yacc_ready")
        out_ready = sem("out_ready")
        out_done = sem("out_done")

        ax_banks = tr + [PG[:, 0, :], PG[:, 1, :]]
        AX_BANK, AX_USE = (0, 1, 2, 3, 0, 1, 0, 1, 2, 3), (0, 0, 0, 0, 1, 1, 2, 2, 1, 1)
        AX_T, AX_F = len(AX_BANK), [AX_BANK.count(b) for b in range(4)]

        def use_wait(eng, u):
            eng.wait_ge(landed[slot_of[u]], 16 * (u // SLOTS + 1))

        def variants(eng, n, emit, widths=NVAR):
            if len(widths) == 1:
                emit(widths[0])
                return
            half = len(widths) // 2
            with eng.If(n > widths[half - 1]):
                variants(eng, n, emit, widths[half:])
            with eng.Else():
                variants(eng, n, emit, widths[:half])

        def blocks(n):
            return [(j, min(P, n - j * P)) for j in range((n + P - 1) // P)]

        def gate_up_of(m, u):
            w = SW if m > 32 else P
            if m == P:
                return PG[:, u % 2, 0:w], PG[:, u % 2, w:2 * w], slice(0, P), w
            return PG[0:P // 2, u % 2, 0:w], PG[P // 2:P, u % 2, 0:w], slice(P // 2, P), w

        def turned_of(m, u):
            bank = tr[u % 2]
            if m == 32:
                return bank[:, P // 2:P].rearrange("p (f t) -> p f t", f=2)
            return bank[:, 0:2 * P].rearrange("p (f t) -> p f t", f=2)[:, :, P - m:P]

        def units(n):
            bl = blocks(n)
            return [(s * len(bl) + j, s, j, m) for s in range(STAGES) for j, m in bl]

        def outputs(j, m):
            if m == P:
                return [(Y[:, 2 * j + h, :], h * 512, 512) for h in range(2)]
            n = P // m
            w = D // n
            return [(Y[i * m:(i + 1) * m, 2 * j + 2 * i // n, 0:w], i * w, w) for i in range(n)]

        def at_unit(e, n, u):
            return e * FT + (FT + (u + 1) * (2 // len(blocks(n))))

        def at_own(e, n, u):
            return e * FT + (u + 1) * (2 // len(blocks(n)))

        def pj_done(name, l):
            return pj_free[PJ.bank((name, l))], PJ.before((name, l)) + 1

        def sc_done(kind, i, l):
            name = ((kind, i), l)
            return sc_free[SC.bank(name)], SC.before(name) + 1

        def tr_done(*name):
            name = name if len(name) > 1 else name[0]
            return tr_free[TR.bank(name)], TR.before(name) + 1

        tr_before_experts = [TR.before(x) + 1 for x in ("router", "rank")]
        if TR.bank("router"):
            tr_before_experts.reverse()

        block = ctx.enter_context(nc.Block())

        @block.sync
        def _(sp):
            w_in, w_out = ap["w_in"], ap["w_out"]

            def cols(w, c, n):
                return w[:, c:c + n].rearrange("(k p) c -> p k c", p=P)

            def rows(w, s):
                return w[s * 2 * P:(s + 1) * 2 * P, :].rearrange("(f p) c -> p f c", p=P)

            def last_reader(kind, a, b):
                if kind == "ada":
                    return tr_full, TR.full(("ada", a, b // 4))
                if kind == "in":
                    return pj_full, PJ.full((IN_ITEM[b], a))
                if kind == "out":
                    return (y_full, 2 + a) if b == D // SW - 1 else (out_read, (D // SW - 1) * a + b + 1)
                return (down_done if kind == "down" else gu_full), 2 * b + 2

            for u, (kind, a, b) in enumerate(uses):
                if u >= SLOTS:
                    sp.wait_ge(*last_reader(*uses[u - SLOTS]))
                slot = ring[:, slot_of[u], :, :]
                if kind == "ada":
                    src = cols(ap["w_ada"][a // 2, a % 2], b * SW, SW)
                elif kind == "in":
                    src = cols(w_in[a], b[0], b[1])
                    slot = slot[:, :, 0:b[1]]
                elif kind == "out":
                    src = cols(w_out[a], b * SW, SW)
                elif kind == "gate":
                    src = cols(ap["w_gate_d"][0], b * SW, SW)
                elif kind == "up":
                    src = cols(ap["w_up_d"][0], b * SW, SW)
                else:
                    src = rows(ap["w_down_d"][0], b)
                    slot = slot.rearrange("p k c -> p (k c)").rearrange("p (f c) -> p f c", f=2)
                sp.dma_start(slot, src).then_inc(landed[slot_of[u]], 16)

            wge = ap["w_gate_e"].rearrange("l e d f -> (l e d) f")
            wue = ap["w_up_e"].rearrange("l e d f -> (l e d) f")
            wde = ap["w_down_e"].rearrange("l e f d -> (l e f) d")

            def expert_use(i, e):
                kind, s = expert_list[i]
                slot = ring_e[i % SLOTS_E]
                if kind == "down":
                    src = wde[bass.ds(e * FF + s * 2 * P, 2 * P), :].rearrange("(f p) c -> p f c", p=P)
                    slot = slot.rearrange("p k c -> p (k c)").rearrange("p (f c) -> p f c", f=2)
                else:
                    w = wge if kind == "gate" else wue
                    src = w[bass.ds(e * D, D), s * SW:(s + 1) * SW].rearrange("(k p) c -> p k c", p=P)
                sp.dma_start(slot, src).then_inc(landed_e[i % SLOTS_E], 16)

            def last_use(i, e):
                kind, s = expert_list[(i - SLOTS_E) % USES]
                return down_done if kind == "down" else gu_full, e * FT + ((FT if i >= SLOTS_E else 0) + 2 * s + 2)

            for i in range(EARLY):
                sp.wait_ge(*last_reader(*uses[n_before - SLOTS + i]))
                expert_use(i, 0)
            sp.wait_ge(y_full, 3)
            with sp.Fori(0, NE - 1) as e:
                for i in range(EARLY, USES):
                    sp.wait_ge(*last_use(i, e))
                    expert_use(i, e)
                for i in range(EARLY):
                    sp.wait_ge(*last_use(i, e + 1))
                    expert_use(i, e + 1)
            for i in range(EARLY, USES):
                sp.wait_ge(*last_use(i, NE - 1))
                expert_use(i, NE - 1)
            sp.wait_ge(out_ready, 4)
            sp.dma_start(out[0].rearrange("(b p) d -> p b d", p=P), tok[:, :, :]).then_inc(out_done, 16)
            sp.wait_ge(out_done, 16)

        @block.tensor
        def _(pe):
            mm = nc.tensor.matmul

            def take_pj(name):
                b = PJ.bank(name)
                if PJ.before(name):
                    pe.wait_ge(pj_free[b], PJ.before(name))
                return pj[b]

            def take_sc(name):
                b = SC.bank(name)
                if SC.before(name):
                    pe.wait_ge(sc_free[b], SC.before(name))
                return sc[b]

            def take_tr(name):
                b = TR.bank(name)
                if TR.before(name):
                    pe.wait_ge(tr_free[b], TR.before(name))
                return tr[b]

            def stats(kind, n, q):
                bank = take_tr((kind, n, "partial"))
                for k in range(KD):
                    if k % 2 == 0:
                        pe.wait_ge(sq_ready, 4 * q + k // 2 + 1)
                    g = 32 * (k % 4)
                    last = mm(bank[g:g + 32, 0:T], ones[:, 0:32], scr[:, k, :], start=(k < 4), stop=(k >= 4))
                last.then_inc(tr_full, 1)
                bank = take_tr((kind, n, "total"))
                pe.wait_ge(*tr_done(kind, n, "partial"))
                for b in range(TB):
                    last = mm(bank[:, b:b + 1], s4[:, b * P:(b + 1) * P], ones[:, 0:1], start=True, stop=True)
                last.then_inc(tr_full, 1)
                bank = take_tr((kind, n, "laid"))
                pe.wait_ge(diag_ready, q + 1)
                for b in range(TB):
                    last = mm(bank[:, b * P:(b + 1) * P], ones[:, :], diag[:, b, :], start=True, stop=True)
                last.then_inc(tr_full, 1)

            def ada_rows(third):
                if third is None:
                    return
                bank = take_tr(("ada", *third))
                us = [use_at[("ada", third[0], 4 * third[1] + c)] for c in range(4)]
                for u in us:
                    use_wait(pe, u)
                for k in range(KD):
                    for c, u in enumerate(us):
                        last = mm(bank[32 * c:32 * c + 32, 0:SW], ccol[:, k, :], ring[:, slot_of[u], k, :],
                                  start=(k == 0), stop=(k == KD - 1))
                last.then_inc(tr_full, 1)

            def ada_columns(third):
                if third is None:
                    return
                bank = take_tr(("adat", *third))
                pe.wait_ge(*tr_done("ada", *third))
                for j in range(2):
                    last = nc.tensor.transpose(bank[:, j * P:(j + 1) * P],
                                               arow[:, ROW_SLOT[third], j * P:(j + 1) * P], ident)
                last.then_inc(tr_full, 1)

            def stats_pre(n, q):
                ada_rows(ADA_NORM[n])
                stats("pre", n, q)
                ada_columns(ADA_NORM[n])

            def gu_tile(slots, half, tile):
                bank = PG[:, tile % 2, :]
                for m in range(2):
                    for k in range(KD):
                        if tile == 0 and m == 0:
                            pe.wait_ge(h_ready, KD + k + 1)
                        last = mm(bank[:, m * T:(m + 1) * T], ring[:, slots[m], k, half * P:(half + 1) * P],
                                  hT[:, k, :], start=(k == 0), stop=(k == KD - 1))
                return last

            def down_tile(slot, half, tile):
                w = ring[:, slot, :, :].rearrange("p k c -> p (k c)").rearrange("p (f c) -> p f c", f=2)
                for k in range(KD):
                    last = mm(Yk[:, k, :], w[:, half, k * P:(k + 1) * P], act[:, tile % 2, :],
                              start=(tile == 0 and k % 2 == 0), stop=(tile == FT - 1), skip_group_check=True)
                return last

            def mixer(l):
                def slot(name, c):
                    u = use_at[(name, l, c)]
                    use_wait(pe, u)
                    return slot_of[u]

                def fm(bank_part, s, c, m):
                    for k in range(KD):
                        last = mm(bank_part, ring[:, s, k, c:c + m], hT[:, k, :], start=(k == 0), stop=(k == KD - 1))
                    return last

                def tm(bank_part, s, b, m, first=False):
                    for k in range(KD):
                        if first:
                            pe.wait_ge(h_ready, KD * 2 * l + k + 1)
                        last = mm(bank_part, hT[:, k, b * P:(b + 1) * P], ring[:, s, k, 0:m],
                                  start=(k == 0), stop=(k == KD - 1))
                    return last

                def fm_pair(name, key, n=2):
                    bank = take_pj((name, l))
                    s = slot("in", key)
                    for i in range(n):
                        last = fm(bank[:, i * T:(i + 1) * T], s, i * P, P)
                    last.then_inc(pj_full, 1)
                    return last

                def a_unit(h, b):
                    u = 2 * h + b
                    bank = take_sc((("a", u), l))
                    keys = (b + 1) * P
                    r = slice(AQ * h, AQ * (h + 1))
                    for j in range(2):
                        mm(bank[:, j * T:j * T + keys], qkA[r, j, b * P:(b + 1) * P], qkA[r, 2 + j, 0:keys],
                           start=True, stop=False)
                        last = mm(bank[:, j * T + b * P:j * T + keys], con[AQ * h:AQ * h + 1, C_MU:C_MU + P],
                                  con[AQ * h:AQ * h + 1, C_MK:C_MK + P], start=False, stop=True)
                    last.then_inc(sc_full, 1)

                def c_unit(u):
                    p, b = u // 2, u % 2
                    bank = take_sc((("c", u), l))
                    keys = (b + 1) * P
                    for j in range(2):
                        mm(bank[:, j * T:j * T + keys], qall[0:CN + CR, 2 * p + j, b * P:(b + 1) * P],
                           kall[0:CN + CR, 2 * p + j, 0:keys], start=True, stop=False)
                        last = mm(bank[:, j * T + b * P:j * T + keys], con[0:1, C_MU:C_MU + P],
                                  con[0:1, C_MK:C_MK + P], start=False, stop=True)
                    last.then_inc(sc_full, 1)

                def at(h):
                    bank = take_tr((f"at{h}", l))
                    pe.wait_ge(combined, AH * l + h + 1)
                    for i in range(3):
                        last = nc.tensor.transpose(bank[:, i * P:(i + 1) * P], aA[:, h % 2, i * P:(i + 1) * P], ident)
                    last.then_inc(tr_full, 1)

                def pt(u):
                    p, b = u // 2, u % 2
                    bank = take_tr((f"pt{u}", l))
                    pe.wait_ge(*sc_done("c", u, l))
                    for j in range(2):
                        for kb in range(b + 1):
                            i = j * (b + 1) + kb
                            last = nc.tensor.transpose(bank[:, i * P:(i + 1) * P],
                                                       E[:, u % 4, j * T + kb * P:j * T + (kb + 1) * P], ident)
                    last.then_inc(tr_full, 1)

                keys = W_IN_ORDER
                s0, s1 = slot("in", keys[0]), slot("in", keys[1])
                for b in range(TB):
                    bank = take_pj((f"lat{b}", l))
                    tm(bank[:, 0:SW], s0, b, SW, first=(b == 0))
                    last = tm(bank[:, SW:LATW], s1, b, LATW - SW)
                    last.then_inc(pj_full, 1)
                fm_pair("a0", keys[2])
                fm_pair("a1", keys[3])
                bank = take_pj(("va", l))
                s = slot("in", keys[4])
                for b in range(TB):
                    last = tm(bank[:, b * T:(b + 1) * T], s, b, SW)
                last.then_inc(pj_full, 1)
                ada_rows(ADA_MIXER[l][0])
                bank = take_tr(("lx", l))
                pe.wait_ge(latn_ready, l + 1)
                pe.wait_ge(kr_ready, l + 1)
                for i in range(2):
                    for b in range(TB):
                        last = nc.tensor.transpose(bank[:, i * T + b * P:i * T + (b + 1) * P],
                                                   latn[:, b, i * P:(i + 1) * P], ident)
                last.then_inc(tr_full, 1)
                bank = take_tr(("lz", l))
                for b in range(TB):
                    nc.tensor.transpose(bank[0:96, b * P:(b + 1) * P], latn[:, b, 256:352], ident)
                    last = nc.tensor.transpose(bank[0:BH, T + b * P:T + (b + 1) * P], lat[:, b, 0:BH], ident)
                last.then_inc(tr_full, 1)
                bank = take_tr(("lf", l))
                for b in range(TB):
                    last = nc.tensor.transpose(bank[0:BH, b * P:(b + 1) * P], lat[:, b, BH:2 * BH], ident)
                last.then_inc(tr_full, 1)
                ada_columns(ADA_MIXER[l][0])
                fm_pair("qk0", keys[5])
                pe.wait_ge(*pj_done("a0", l))
                pe.wait_ge(*pj_done("a1", l))
                a_unit(0, 0)
                a_unit(0, 1)
                pe.wait_ge(*tr_done("lx", l))
                pe.wait_ge(*tr_done("lz", l))
                pe.wait_ge(wl_in, 48 * (l + 1))
                for p in range(3):
                    bank = take_pj((f"uq{p}", l))
                    for j in range(2):
                        c = (2 * p + j) * (CN + CR)
                        mm(bank[0:96, j * T:(j + 1) * T], wuq[:, 0, c:c + 96], cqT[:, :], start=True, stop=False)
                        last = mm(bank[0:96, j * T:(j + 1) * T], wuq[0:64, 1, c:c + 96], zT[0:64, :],
                                  start=False, stop=True)
                    last.then_inc(pj_full, 1)
                for p in range(3):
                    bank = take_pj((f"uk{p}", l))
                    for j in range(2):
                        c = (2 * p + j) * (CN + CV)
                        last = mm(bank[0:CN, j * T:(j + 1) * T], wukv[:, c:c + CN], ckT[:, :], start=True, stop=True)
                    last.then_inc(pj_full, 1)
                wv = wukv.rearrange("p (h c) -> p h c", h=CH)[:, :, CN:CN + CV]
                for b in range(TB):
                    bank = take_pj((f"uv{b}", l))
                    last = mm(bank[:, 0:CH * CV].rearrange("p (h c) -> p h c", h=CH), ckT[:, b * P:(b + 1) * P], wv,
                              start=True, stop=True)
                    last.then_inc(pj_full, 1)
                a_unit(1, 0)
                a_unit(1, 1)
                fm_pair("qk1", keys[6])
                for h in range(2, AH):
                    for b in range(TB):
                        a_unit(h, b)
                fm_pair("qk2", keys[7])
                rot = con[CN:CN + CR, C_ROT:C_ROT + CR]
                pe.wait_ge(*pj_done("uq1", l))
                pe.wait_ge(*pj_done("uq2", l))
                for i in range(4):
                    bank = take_sc((("rot", i), l))
                    src = qall[CN:CN + CR, 2 * i:2 * i + 2, :].rearrange("p h t -> p (h t)") if i < 3 else zT[CN:CN + CR, :]
                    n = 2 * T if i < 3 else T
                    mm(bank[CN:CN + CR, 0:n], rot, src, start=True, stop=True).then_inc(sc_full, 1)
                ada_rows(ADA_MIXER[l][1])
                at(0)
                at(1)
                fm_pair("ob0", keys[8])
                fm_pair("ob1", keys[9], 1)
                ada_columns(ADA_MIXER[l][1])
                at(2)
                at(3)
                pe.wait_ge(rope_done, l + 1)
                pe.wait_ge(*pj_done("uk1", l))
                pe.wait_ge(*pj_done("uk2", l))
                pe.wait_ge(*sc_done("rot", 2, l))
                for u in range(4):
                    c_unit(u)
                bank = take_tr(("ao", l))
                pe.wait_ge(*tr_done("at2", l))
                pe.wait_ge(*tr_done("at3", l))
                pe.wait_ge(*pj_done("va", l))
                for b in range(TB):
                    for h in range(AH):
                        o = bank[:, (b * AH + h) * AV:(b * AH + h + 1) * AV]
                        for kb in range(b + 1):
                            last = mm(o, aT[:, h, (b + kb) * P:(b + kb + 1) * P], va[:, kb, h * AV:(h + 1) * AV],
                                      start=(kb == 0), stop=(kb == b))
                last.then_inc(tr_full, 1)
                s0, s1 = slot("in", keys[10]), slot("in", keys[11])
                for b in range(TB):
                    bank = take_pj((f"vb{b}", l))
                    tm(bank[:, 0:SW], s0, b, SW)
                    tm(bank[:, SW:SW + P], s1, b, P).then_inc(pj_full, 1)
                pt(0)
                c_unit(4)
                pt(1)
                c_unit(5)
                for u in range(2, 6):
                    pt(u)
                ada_rows(ADA_MIXER[l][2])
                bank = take_tr(("gt", l))
                pe.wait_ge(gates_ready, l + 1)
                for i, g in enumerate((g_a, g_b)):
                    for b in range(TB):
                        c = (i * TB + b) * BH
                        last = nc.tensor.transpose(bank[:, c:c + BH], g[0:BH, b * P:(b + 1) * P], ident[0:BH, 0:BH])
                last.then_inc(tr_full, 1)
                pe.wait_ge(qks_ready, l + 1)
                for h in range(BH):
                    bank = take_sc((("w", h), l))
                    sel = ident[0:BH, h:h + 1].to_broadcast([BH, P])
                    mm(bank[:, 0:T], sel, g_m[0:BH, :], start=True, stop=False, skip_group_check=True)
                    mm(bank[:, T:T + P], sel, g_m[0:BH, P:T], start=False, stop=False, skip_group_check=True)
                    mm(bank[:, 0:P], ident, caus, start=False, stop=False, skip_group_check=True)
                    mm(bank[:, T:T + P], ident, caus, start=False, stop=True,
                       skip_group_check=True).then_inc(sc_full, 1)
                    bank = take_sc((("s", h), l))
                    r = slice(BD * (h % 2), BD * (h % 2) + BD)
                    mm(bank[:, 0:T], qks[r, 3 + h // 2, 0:P], qks[r, h // 2, :], start=True, stop=True)
                    mm(bank[:, T:T + P], qks[r, 3 + h // 2, P:T], qks[r, h // 2, P:T],
                       start=True, stop=True).then_inc(sc_full, 1)
                ada_columns(ADA_MIXER[l][2])
                pe.wait_ge(*tr_done("pt4", l))
                pe.wait_ge(*tr_done("pt5", l))
                pe.wait_ge(*pj_done("uv0", l))
                pe.wait_ge(*pj_done("uv1", l))
                for b in range(TB):
                    bank = take_tr((f"co{b}", l))
                    for h in range(CH):
                        for kb in range(b + 1):
                            c = (2 * b + (h % 2) * (b + 1) + kb) * P
                            last = mm(bank[:, h * CV:(h + 1) * CV], PT[:, h // 2, c:c + P],
                                      vc[:, kb, h * CV:(h + 1) * CV], start=(kb == 0), stop=(kb == b))
                    last.then_inc(tr_full, 1)
                pe.wait_ge(*sc_done("s", BH - 2, l))
                pe.wait_ge(*sc_done("s", BH - 1, l))
                pe.wait_ge(*pj_done("vb0", l))
                pe.wait_ge(*pj_done("vb1", l))
                for b in range(TB):
                    bank = take_tr((f"bo{b}", l))
                    for h in range(BH):
                        o = bank[:, h * (BD + 1):(h + 1) * (BD + 1)]
                        for kb in range(b + 1):
                            c = kb * T if kb == b else P
                            last = mm(o, scw[:, h, c:c + P], vbx[:, kb, h, :], start=(kb == 0), stop=(kb == b))
                    last.then_inc(tr_full, 1)
                ada_rows(ADA_MIXER[l][3])
                for i in range(4):
                    bank = take_tr((f"mt{i}", l))
                    if i == 0:
                        pe.wait_ge(tok_ready, l + 1)
                    for j in range(2):
                        for b in range(TB):
                            f = 2 * i + j
                            last = nc.tensor.transpose(bank[:, j * T + b * P:j * T + (b + 1) * P],
                                                       tok[:, b, f * P:(f + 1) * P], ident)
                    last.then_inc(tr_full, 1)
                ada_columns(ADA_MIXER[l][3])
                pe.wait_ge(*tr_done("mt2", l))
                pe.wait_ge(*tr_done("mt3", l))
                for b in range(2):
                    pe.wait_ge(pj_free[b], len(PJ_LAYER) // 2 * (l + 1))
                for b in range(4):
                    pe.wait_ge(sc_free[b], len([i for i in range(len(SC_LAYER) * (l + 1)) if i % 4 == b]))
                for c in range(D // SW):
                    s = slot("out", c)
                    for j in range(2):
                        for k in range(KD):
                            last = mm(Yk[:, 2 * c + j, :], ring[:, s, k, j * P:(j + 1) * P], mixT[:, k, :],
                                      start=(k == 0), stop=(k == KD - 1))
                    last.then_inc(out_read if c < D // SW - 1 else y_full, 1)

            pe.wait_ge(const_set, 3)
            pe.wait_ge(x_in, 32)
            for k in range(KD):
                for b in range(TB):
                    last = nc.tensor.transpose(Yk[:, k, b * P:(b + 1) * P], tok[:, b, k * P:(k + 1) * P], ident)
            last.then_inc(y_full, 1)
            stats_pre(0, 0)
            pe.wait_ge(param_in, 16 * n_param)
            for i, (name, m) in enumerate((("param1", 124), ("param2", 112))):
                bank = take_tr(name)
                nc.tensor.transpose(bank[:, 0:m], prow[0:m, i, :], ident[0:m, 0:m]).then_inc(tr_full, 1)
            bank = take_tr("lam")
            pe.wait_ge(lam_prod, 2)
            mm(bank[:, 0:2 * L], ones[0:AQ, :], lam_pr[:, :, :].rearrange("p a l -> p (a l)"),
               start=True, stop=True).then_inc(tr_full, 1)
            pe.wait_ge(ccol_ready, 1)
            for third in ADA_START:
                ada_rows(third)
            for third in ADA_START:
                ada_columns(third)

            mixer(0)
            stats("post", 0, 1)
            stats_pre(1, 2)
            for t in range(FT + 1):
                if t < FT:
                    s, half = t // 2, t % 2
                    us = [use_at[("gate", 0, s)], use_at[("up", 0, s)]]
                    for u in us:
                        use_wait(pe, u)
                    if t >= 2:
                        pe.wait_ge(act_ready, t - 1)
                    gu_tile([slot_of[u] for u in us], half, t).then_inc(gu_full, 1)
                if t == 3:
                    ada_columns(ADA_DENSE)
                if t >= 1:
                    s, half = (t - 1) // 2, (t - 1) % 2
                    u = use_at[("down", 0, s)]
                    use_wait(pe, u)
                    pe.wait_ge(act_ready, t)
                    down_tile(slot_of[u], half, t - 1).then_inc(down_done, 1)
                if t == 2:
                    ada_rows(ADA_DENSE)
            stats("post", 1, 3)

            stats_pre(2, 4)
            mixer(1)
            stats("post", 2, 5)
            stats_pre(3, 6)
            bank = take_tr("router")
            for b in range(TB):
                for k in range(KD):
                    if b == 0:
                        pe.wait_ge(h_ready, 3 * KD + k + 1)
                    last = mm(bank[:, b * NE:(b + 1) * NE], hT[:, k, b * P:(b + 1) * P], wr[:, k, :],
                              start=(k == 0), stop=(k == KD - 1))
            last.then_inc(tr_full, 1)
            for k in range(KD):
                for b in range(TB):
                    last = nc.tensor.transpose(Y[:, 2 * b + k // 4, (k % 4) * P:(k % 4 + 1) * P],
                                               hT[:, k, b * P:(b + 1) * P], ident)
            last.then_inc(y_full, 1)
            bank = take_tr("rank")
            pe.wait_ge(routed, 1)
            mm(bank[:, 0:NE], tri, Mm[:, 0, 0:NE], start=True, stop=True)
            mm(bank[:, NE:2 * NE], ones[:, :], Mm[:, 0, 0:NE], start=True, stop=False)
            mm(bank[:, NE:2 * NE], tri, Mm[:, 1, 0:NE], start=False, stop=True)
            mm(bank[:, 2 * NE:3 * NE], ones[:, :], Mm[:, 0, 0:NE], start=True, stop=False)
            mm(bank[:, 2 * NE:3 * NE], ones[:, :], Mm[:, 1, 0:NE], start=False, stop=True).then_inc(tr_full, 1)
            pe.wait_ge(htok_ready, 4)
            for b in range(2):
                pe.wait_ge(tr_free[b], tr_before_experts[b])

            for b in range(4):
                pe.sem_inc(ax_free[b], AX_F[b])
            with pe.Fori(0, NE) as e:
                n_tok = pe.value_load(cnt[0:1, bass.ds(e, 1)], min_val=0, max_val=T)

                def expert(n):
                    ax = [0]

                    def take():
                        i = ax[0]
                        ax[0] += 1
                        b = AX_BANK[i]
                        pe.wait_ge(ax_free[b], e * AX_F[b] + (AX_F[b] + AX_USE[i]))
                        return ax_banks[b]

                    pe.wait_ge(hot_ready, e * 1 + 1)
                    for i in range(4):
                        bank = take()
                        for j in range(2):
                            k = 2 * i + j
                            for b in range(TB):
                                w = max(n, P)
                                last = mm(bank[:, j * T:j * T + w], tok[:, b, k * P:(k + 1) * P], oh[:, b, 0:w],
                                          start=(b == 0), stop=(b == TB - 1))
                        last.then_inc(ax_full, 1)
                    for b in range(TB):
                        bank = take()
                        for j, m in blocks(n):
                            last = nc.tensor.transpose(bank[:, j * P:(j + 1) * P], ohg[:, b, j * P:(j + 1) * P], ident)
                        last.then_inc(ax_full, 1)
                    for b in range(4):
                        pe.wait_ge(ax_free[b], e * AX_F[b] + (AX_F[b] + 1))

                    step = 2 // len(blocks(n))

                    def weights(kind, s):
                        i = expert_at[kind, s]
                        pe.wait_ge(landed_e[i % SLOTS_E], e * (16 * USES // SLOTS_E) + 16 * (i // SLOTS_E + 1))
                        return ring_e[i % SLOTS_E]

                    def gate_up(u, s, j, m):
                        w = [weights("gate", s), weights("up", s)]
                        if u >= 2:
                            pe.wait_ge(act_ready, at_unit(e, n, u - 2))
                        bank = PG[:, u % 2, :]
                        x = mixT[:, :, j * P:j * P + m]
                        if m < P:
                            width = gate_up_of(m, u)[3]
                            for k in range(KD):
                                for i in range(P // m):
                                    c = i * width
                                    last = mm(bank[i * m:(i + 1) * m, 0:width], x[:, k, :],
                                              w[c // SW][:, k, c % SW:c % SW + width],
                                              start=(k == 0), stop=(k == KD - 1))
                        else:
                            for i in range(2):
                                for k in range(KD):
                                    last = mm(bank[:, i * SW:(i + 1) * SW], x[:, k, :], w[i][:, k, :],
                                              start=(k == 0), stop=(k == KD - 1))
                        last.then_inc(gu_full, step)

                    def turn(u, s, j, m):
                        pe.wait_ge(act_ready, at_unit(e, n, u))
                        if u >= 2:
                            pe.wait_ge(at_ready, at_own(e, n, u - 2))
                        r, width = gate_up_of(m, u)[2:]
                        for f in range(width // P):
                            last = mm(tr[u % 2][:, f * P:(f + 1) * P], actK[r, u % 2, f * P:(f + 1) * P], ident[r, :],
                                      start=True, stop=True)
                        last.then_inc(tp_full, step)

                    def down(u, s, j, m):
                        w = weights("down", s).rearrange("p k c -> p (k c)").rearrange("p (f c) -> p f c", f=2)
                        pe.wait_ge(at_ready, at_own(e, n, u))
                        for f in range(2):
                            for o, c, width in outputs(j, m):
                                last = mm(o, actT[:, u % 2, f, 0:m], w[:, f, c:c + width],
                                          start=(s == 0 and f == 0), stop=(s == STAGES - 1 and f == 1))
                        last.then_inc(down_done, step)

                    us = units(n)
                    for i in range(len(us) + 2):
                        if i < len(us):
                            gate_up(*us[i])
                        if i == 0:
                            for b in range(2):
                                pe.wait_ge(ax_free[b], e * AX_F[b] + (AX_F[b] + 2))
                        if 1 <= i <= len(us):
                            turn(*us[i - 1])
                        if i >= 2:
                            down(*us[i - 2])
                    pe.wait_ge(ye_ready, e * 2 + 2)
                    for i in range(4):
                        bank = take()
                        bl = blocks(n)
                        for q in range(2):
                            k = 2 * i + q
                            for j, m in bl:
                                last = mm(bank[:, q * T:(q + 1) * T], yeK[0:m, j, k * P:(k + 1) * P], gPT[0:m, j, :],
                                          start=(j == 0), stop=(j == len(bl) - 1))
                        last.then_inc(ax_full, 1)
                    assert ax[0] == AX_T

                variants(pe, n_tok, expert)

            for b in range(4):
                pe.wait_ge(ax_free[b], (NE + 1) * AX_F[b])
            stats("post", 3, 7)
            pe.wait_ge(x_upd, 4 * KD // 2)
            pe.wait_ge(x_updv, 4 * KD // 2)
            for k in range(KD):
                for b in range(TB):
                    last = nc.tensor.transpose(Y[:, 2 * b + k // 4, (k % 4) * P:(k % 4 + 1) * P],
                                               xT[:, k, b * P:(b + 1) * P], ident)
            last.then_inc(y_full, 1)

        @block.scalar
        def _(act_e):
            ae = act_e

            def run(out_, in_, func, **kw):
                return nc.scalar.activation(out_, in_, func, **kw)

            def load_latent_weights(l):
                ae.dma_start(wuq[:, 0, :], ap["w_uq"][l, 0:P, :]).then_inc(wl_in, 16)
                ae.dma_start(wuq[0:CQL - P, 1, :], ap["w_uq"][l, P:CQL, :]).then_inc(wl_in, 16)
                ae.dma_start(wukv, ap["w_ukv"][l]).then_inc(wl_in, 16)

            def squares_pre(n):
                for j in range(4):
                    if n == 0:
                        ae.wait_ge(y_quarter, j + 1)
                    else:
                        ae.wait_ge(x_upd if j < 2 else x_updv, KD // 2 * (n - 1) + 2 * (j % 2) + 2)
                    run(scr[:, 2 * j:2 * j + 2, :], xT[:, 2 * j:2 * j + 2, :], ACT.Square).then_inc(sq_ready, 1)

            def shift(n):
                for k in range(KD):
                    ae.wait_ge(hx_ready, KD * n + k + 1)
                    run(hT[:, k, :], hT[:, k, :], ACT.Identity, bias=mod[:, n, k:k + 1]).then_inc(h_ready, 1)

            def squares_post(n, ready, value):
                ae.wait_ge(ready, value)
                for j in range(4):
                    src = yacc[:, 2 * j:2 * j + 2, :] if n == 3 else Yk[:, 2 * j:2 * j + 2, :]
                    run(scr[:, 2 * j:2 * j + 2, :], src, ACT.Square).then_inc(sq_ready, 1)

            def ada_rows(third):
                if third is None:
                    return
                name = ("ada", *third)
                ae.wait_ge(tr_full, TR.full(name))
                run(arow[:, ROW_SLOT[third], :], tr[TR.bank(name)][:, 0:SW], ACT.Copy).then_inc(tr_free[TR.bank(name)], 1)

            def mixer(l):
                def pj_item(name):
                    ae.wait_ge(pj_full, PJ.full((name, l)))
                    return pj[PJ.bank((name, l))], pj_free[PJ.bank((name, l))]

                def tr_item(name):
                    ae.wait_ge(tr_full, TR.full((name, l)))
                    return tr[TR.bank((name, l))], tr_free[TR.bank((name, l))]

                def exps(kind, u):
                    i = u if kind == "a" else 8 + u
                    ae.wait_ge(negmax, 14 * l + i + 1)
                    if kind == "a" and u >= 4:
                        ae.wait_ge(combined, AH * l + (u - 4) // 2 + 1)
                    if kind == "c" and u < 4:
                        ae.wait_ge(combined, AH * l + (u + 4) // 2 + 1)
                    if kind == "c" and u >= 4:
                        ae.wait_ge(tr_full, TR.full((f"pt{u - 4}", l)))
                    name = ((kind, u), l)
                    bank, keys = sc[SC.bank(name)], (u % 2 + 1) * P
                    for j in range(2):
                        last = run(E[:, i % 4, j * T:j * T + keys], bank[:, j * T:j * T + keys], ACT.Exp,
                                   bias=nm[:, i, j:j + 1], accum_out=se[:, i, j:j + 1])
                    last.then_inc(sc_free[SC.bank(name)], 1)

                for b in range(TB):
                    bank, free = pj_item(f"lat{b}")
                    run(lat[:, b, :], bank[:, 0:LATW], ACT.Copy)
                    o = 3 * P * b
                    run(sqj[:, o:o + CQL], bank[:, 12:12 + CQL], ACT.Square, scale=CQL ** -0.5, accum_out=ss[:, b:b + 1])
                    run(sqj[:, o + CQL:o + CQL + CKV], bank[:, 12 + CQL:12 + CQL + CKV], ACT.Square,
                        scale=CKV ** -0.5, accum_out=ss[:, 2 + b:3 + b]).then_inc(free, 1)
                bank, free = pj_item("a0")
                run(qkA[:, 0:2, :], bank.rearrange("p (a t) -> p a t", a=2), ACT.Copy, scale=SC_A).then_inc(free, 1)

                def raw_pair(i):
                    bank, free = pj_item(f"qk{i}")
                    run(raw[:, 2 * i:2 * i + 2, CW - 1:], bank.rearrange("p (a t) -> p a t", a=2), ACT.Copy).then_inc(free, 1)

                ada_rows(ADA_MIXER[l][0])
                raw_pair(0)
                exps("a", 0)
                exps("a", 1)
                for p in range(3):
                    bank, free = pj_item(f"uq{p}")
                    run(qall[0:96, 2 * p:2 * p + 2, :], bank[0:96, :].rearrange("p (a t) -> p a t", a=2), ACT.Copy,
                        scale=SC_C).then_inc(free, 1)
                exps("a", 2)
                exps("a", 3)
                raw_pair(1)
                ae.wait_ge(gate_in, l + 1)
                run(g_e[0:BH, :], g_n[0:BH, :], ACT.Exp).then_inc(gate_exp, 1)
                ae.wait_ge(gate_exp, l + 1)
                run(g_e[0:BH, :], g_e[0:BH, :], ACT.Ln, bias=1.0).then_inc(gate_ln, 1)
                for u in range(4, 8):
                    exps("a", u)
                raw_pair(2)

                def at(h):
                    bank, free = tr_item(f"at{h}")
                    run(aT[:, h, :], bank[:, 0:3 * P], ACT.Copy).then_inc(free, 1)

                ada_rows(ADA_MIXER[l][1])
                at(0)
                at(1)
                bank, free = pj_item("ob0")
                run(obt[:, 0:2, :], bank.rearrange("p (a t) -> p a t", a=2), ACT.Copy).then_inc(free, 1)
                bank, free = pj_item("ob1")
                run(obt[:, 2, :], bank[:, 0:T], ACT.Copy).then_inc(free, 1)
                at(2)
                at(3)
                ae.wait_ge(conv_ready, l + 1)
                run(qks, cv, ACT.Silu).then_inc(qks_ready, 1)
                ae.wait_ge(*pj_done("ob0", l))
                ae.wait_ge(*pj_done("ob1", l))
                run(obt, obt, ACT.Tanh, scale=0.5).then_inc(obt_tanh, 1)
                for u in range(4):
                    exps("c", u)
                bank = tr[TR.bank(("ao", l))]
                ae.wait_ge(tr_full, TR.full(("ao", l)))
                run(sqj[:, 0:2 * T], bank, ACT.Square).then_inc(ao_sq, 1)

                def pt(u):
                    p, b = u // 2, u % 2
                    bank, free = tr_item(f"pt{u}")
                    o, n = 2 * b * P, 2 * (b + 1) * P
                    run(PT[:, p, o:o + n], bank[:, 0:n], ACT.Copy).then_inc(free, 1)

                pt(0)
                exps("c", 4)
                exps("c", 5)
                pt(2)
                pt(4)
                ada_rows(ADA_MIXER[l][2])
                bank, free = tr_item("gt")
                run(aK[:, :], bank[:, 0:12], ACT.Copy)
                run(em[:, :], bank[:, 12:24], ACT.Exp).then_inc(free, 1)
                ae.wait_ge(*tr_done("gt", l))
                for h in range(BH):
                    name = (("w", h), l)
                    bank = sc[SC.bank(name)]
                    ae.wait_ge(sc_full, SC.full(name))
                    if h >= 2:
                        ae.wait_ge(*sc_done("s", h - 2, l))
                    run(W[:, h % 2, 0:T], bank[:, 0:T], ACT.Exp, bias=aK[:, h:h + 1])
                    run(W[:, h % 2, T:T + P], bank[:, T:T + P], ACT.Exp,
                        bias=aK[:, BH + h:BH + h + 1]).then_inc(sc_free[SC.bank(name)], 1)
                ae.wait_ge(*tr_done("bo0", l))
                ae.wait_ge(*tr_done("bo1", l))
                run(sqj[:, 0:2 * BH * BD].rearrange("p (a d) -> p a d", d=BD), hb, ACT.Square).then_inc(hb_sq, 1)
                ada_rows(ADA_MIXER[l][3])
                bank, free = tr_item("mt0")
                run(mixT[:, 0:2, :], bank.rearrange("p (a t) -> p a t", a=2), ACT.Copy, scale=gd[:, l:l + 1]).then_inc(free, 1)
                bank, free = tr_item("mt3")
                run(mixT[:, 6:8, :], bank.rearrange("p (a t) -> p a t", a=2), ACT.Copy).then_inc(free, 1)

            ae.dma_start(con[:, :], ap["consts"]).then_inc(x_in, 16)
            ae.dma_start(tok[:, :, :], ap["x"][0].rearrange("(b p) d -> p b d", p=P)).then_inc(x_in, 16)
            with nc.allow_non_contiguous_dma(reason="a few hundred single parameters, once"):
                for dst, src in params:
                    ae.dma_start(dst, src).then_inc(param_in, 16)
            load_latent_weights(0)
            ae.wait_ge(y_full, 1)
            for j in range(4):
                run(xT[:, 2 * j:2 * j + 2, :], Yk[:, 2 * j:2 * j + 2, :], ACT.Copy).then_inc(y_quarter, 1)
            squares_pre(0)
            ae.wait_ge(*tr_done("param2"))
            ae.wait_ge(const_set, 3)
            run(ccol[:, :, 0], craw, ACT.Silu).then_inc(ccol_ready, 1)
            ae.wait_ge(tr_full, TR.full("lam"))
            run(lam_e[:, :, :], tr[TR.bank("lam")][:, 0:2 * L].rearrange("p (a l) -> p a l", a=2),
                ACT.Exp).then_inc(tr_free[TR.bank("lam")], 1)
            for third in ADA_START:
                ada_rows(third)
            shift(0)
            ae.wait_ge(rope_in, 2)
            run(sin[CN:CN + CR, :], sin[CN:CN + CR, :], ACT.Sin).then_inc(rope_set, 1)
            run(cos[CN:CN + CR, :], cos[CN:CN + CR, :], ACT.Sin).then_inc(rope_set, 1)
            mixer(0)
            squares_post(0, y_full, 2)
            squares_pre(1)
            ada_rows(ADA_NORM[1])
            shift(1)
            for t in range(FT):
                ae.wait_ge(gu_full, t + 1)
                if t >= 2:
                    ae.wait_ge(act_ready, t - 1)
                run(sg[:, t % 2, :], PG[:, t % 2, 0:T], ACT.Silu).then_inc(silu_done, 1)
                if t == 2:
                    ada_rows(ADA_DENSE)
            squares_post(1, down_done, FT)
            load_latent_weights(1)
            squares_pre(2)
            ada_rows(ADA_NORM[2])
            shift(2)
            mixer(1)
            squares_post(2, y_full, 3)
            squares_pre(3)
            ada_rows(ADA_NORM[3])
            shift(3)
            ae.wait_ge(gap_ready, 1)
            run(gt2[:, :, 1], gt2[:, :, 0], ACT.Exp).then_inc(gap_exp, 1)
            ae.wait_ge(y_full, 4)
            for q in range(4):
                run(tok[:, q // 2, (q % 2) * 512:(q % 2 + 1) * 512], Y[:, q, :], ACT.Copy).then_inc(htok_ready, 1)
            ae.wait_ge(*tr_done("rank"))
            ae.wait_ge(yacc_zero, 1)
            with ae.Fori(0, NE) as e:
                n_tok = ae.value_load(cnt[0:1, bass.ds(e, 1)], min_val=0, max_val=T)

                def expert(n):
                    def item(i):
                        ae.wait_ge(ax_full, e * AX_T + (i + 1))
                        return ax_banks[AX_BANK[i]], ax_free[AX_BANK[i]]

                    for i in (0, 2):
                        bank, free = item(i)
                        run(mixT[:, 2 * i:2 * i + 2, 0:n], bank.rearrange("p (a t) -> p a t", a=2)[:, :, 0:n],
                            ACT.Copy).then_inc(free, 1)
                    bank, free = item(4)
                    for j, m in blocks(n):
                        last = run(gPT[0:m, j, 0:P], bank[0:m, j * P:(j + 1) * P], ACT.Copy)
                    last.then_inc(free, 1)
                    for u, s, j, m in units(n):
                        gate, up, r, width = gate_up_of(m, u)
                        ae.wait_ge(gu_full, at_unit(e, n, u))
                        if u >= 2:
                            ae.wait_ge(act_ready, at_unit(e, n, u - 2))
                        run(sgK[r, u % 2, 0:width], gate, ACT.Silu).then_inc(silu_done, 2 // len(blocks(n)))
                    ae.wait_ge(down_done, e * FT + 2 * FT)
                    for j, m in blocks(n):
                        for piece, c, width in outputs(j, m):
                            if c < D // 2:
                                last = run(yeK[0:m, j, c:c + width], piece, ACT.Copy)
                    last.then_inc(ye_ready, 1)

                variants(ae, n_tok, expert)
            squares_post(3, yacc_ready, 4 * NE)
            ae.wait_ge(y_full, 5)
            for q in range(4):
                run(tok[:, q // 2, (q % 2) * 512:(q % 2 + 1) * 512], Y[:, q, :], ACT.Copy).then_inc(out_ready, 1)

        @block.vector
        def _(ve):
            V = nc.vector
            steps = [0]

            def mark(ins):
                ins.then_inc(dve_seq, 1)
                steps[0] += 1
                return ins

            def settle():
                ve.wait_ge(dve_seq, steps[0])

            def tr_item(*name):
                name = name if len(name) > 1 else name[0]
                ve.wait_ge(tr_full, TR.full(name))
                return tr[TR.bank(name)], tr_free[TR.bank(name)]

            def root(name):
                ve.wait_ge(rstd_ready, RS[name] + 1)
                return rs[:, MS[name], :]

            def mean(kind, n):
                bank, free = tr_item(kind, n, "partial")
                V.tensor_copy(s4[:, :], bank[:, 0:T]).then_inc(free, 1)
                bank, free = tr_item(kind, n, "total")
                V.tensor_scalar(meps[:, :], bank[:, 0:TB], 1.0 / (32 * D), EPS, ALU.mult, ALU.add).then_inc(free, 1)
                ve.wait_ge(rstd_ready, RS[(kind, n)] + 1)
                for b in range(TB):
                    last = V.tensor_scalar(diag[:, b, :], ident, root_[:, b:b + 1], None, ALU.mult)
                last.then_inc(diag_ready, 1)
                bank, free = tr_item(kind, n, "laid")
                V.tensor_copy(rsb[:, :], bank[:, 0:T]).then_inc(free, 1)
                ve.wait_ge(*tr_done(kind, n, "laid"))
                settle()

            def pre(n):
                if n:
                    mean("pre", n)
                    ve.wait_ge(x_upd, KD // 2 * n)
                    ve.wait_ge(x_updv, KD // 2 * n)
                for k in range(KD):
                    V.scalar_tensor_tensor(hT[:, k, :], xT[:, k, :], gs[:, n, k:k + 1], rsb[:, :],
                                           ALU.mult, ALU.mult).then_inc(hx_ready, 1)
                ada(ADA_NORM[n])

            def post(n):
                mean("post", n)
                for k in range(KD):
                    src = yacc[:, k, :] if n == 3 else Yk[:, k, :]
                    V.scalar_tensor_tensor(scr[:, k, :], src, gg[:, n, k:k + 1], rsb[:, :],
                                           ALU.mult, ALU.mult).then_inc(upd_ready, 1)
                for k in range(KD // 2, KD):
                    ve.wait_ge(upd_ready, KD * n + k + 1)
                    V.tensor_tensor(xT[:, k, :], xT[:, k, :], scr[:, k, :], ALU.add).then_inc(x_updv, 1)

            def ada(third):
                if third is None:
                    return
                n, g = third
                bank, free = tr_item("adat", n, g)
                cols = bank[:, 0:2 * P].rearrange("p (j c x) -> p j c x", j=2, c=4)[:, :, :, 0]
                m = slice(g * KD, (g + 1) * KD)
                V.tensor_tensor(mod[:, n, m].rearrange("p (c j) -> p j c", j=2), cols,
                                bada[:, n, m].rearrange("p (c j) -> p j c", j=2), ALU.add).then_inc(free, 1)
                l, s = n // 2, 2 * (n % 2)
                if g:
                    ve.wait_ge(*tr_done("adat", n, g))
                if g == 1:
                    mark(V.scalar_tensor_tensor(gs[:, n, :], mod[:, n, m], 1.0, gn[:, l, s, :], ALU.add, ALU.mult))
                if g == 2:
                    mark(V.tensor_tensor(gg[:, n, :], mod[:, n, m], gn[:, l, s + 1, :], ALU.mult))

            def mixer(l):
                def pj_item(name):
                    ve.wait_ge(pj_full, PJ.full((name, l)))
                    return pj[PJ.bank((name, l))], pj_free[PJ.bank((name, l))]

                def negmaxes(kind, *units):
                    for u in units:
                        name = ((kind, u), l)
                        i, keys = (u if kind == "a" else 8 + u), (u % 2 + 1) * P
                        ve.wait_ge(sc_full, SC.full(name))
                        bank = sc[SC.bank(name)].rearrange("p (a t) -> p a t", a=2)
                        V.tensor_reduce(nm[:, i, :], bank[:, :, 0:keys], AX.X, ALU.max, negate=True).then_inc(negmax, 1)

                def combine(h):
                    for b in range(TB):
                        ve.wait_ge(*sc_done("a", 2 * h + b, l))
                    if h >= 2:
                        ve.wait_ge(tr_full, TR.full((f"at{h - 2}", l)))
                    r = rc[:, 2 * h:2 * h + 2, :]
                    mark(V.reciprocal(r, se[:, 2 * h:2 * h + 2, :]))
                    settle()
                    mark(V.tensor_tensor(r, r, lam_v[:, l:l + 1, :].to_broadcast([P, 2, 2]), ALU.mult))
                    settle()
                    for b in range(TB):
                        u, n = 2 * h + b, (b + 1) * P
                        e2 = E[:, u % 4, T:T + n]
                        mark(V.tensor_scalar(e2, e2, rc[:, u, 1:2], None, ALU.mult))
                    settle()
                    for b in range(TB):
                        u, n = 2 * h + b, (b + 1) * P
                        last = V.scalar_tensor_tensor(aA[:, h % 2, b * P:b * P + n], E[:, u % 4, 0:n], rc[:, u, 0:1],
                                                      E[:, u % 4, T:T + n], ALU.mult, ALU.add)
                    last.then_inc(combined, 1)

                mark(V.memset(raw[:, :, 0:CW - 1], 0.0))
                mark(V.memset(vbx[:, :, :, BD:BD + 1].rearrange("p b h o -> p (b h) o"), 1.0))
                mark(V.memset(scr[:, 7, :], 0.0))
                for b in range(TB):
                    ve.wait_ge(*pj_done(f"lat{b}", l))
                V.tensor_scalar(ms[:, MS[("c", l)], 0:4], ss[:, :], EPS, None, ALU.add).then_inc(mean_ready, 1)
                bank, free = pj_item("a1")
                V.tensor_copy(qkA[:, 2:4, :], bank.rearrange("p (a t) -> p a t", a=2)).then_inc(free, 1)
                bank, free = pj_item("va")
                V.tensor_copy(va, bank.rearrange("p (a t) -> p a t", a=2)).then_inc(free, 1)
                r = root(("c", l))
                for b in range(TB):
                    V.tensor_scalar(latn[:, b, 0:P], lat[:, b, 12:12 + P], r[:, b:b + 1], None, ALU.mult)
                    V.tensor_scalar(latn[:, b, 256:320], lat[:, b, 12 + P:12 + CQL], r[:, b:b + 1], None, ALU.mult)
                    last = V.tensor_scalar(latn[:, b, P:2 * P], lat[:, b, 12 + CQL:12 + CQL + CKV], r[:, 2 + b:3 + b],
                                           None, ALU.mult)
                last.then_inc(latn_ready, 1)
                bank, free = tr_item("lx", l)
                V.tensor_scalar(cqT, bank[:, 0:T], gq[:, l, 0:1], None, ALU.mult)
                V.tensor_scalar(ckT, bank[:, T:2 * T], gkv[:, l:l + 1], None, ALU.mult).then_inc(free, 1)
                bank, free = tr_item("lz", l)
                V.tensor_scalar(zT[0:64, :], bank[0:64, 0:T], gq[0:64, l, 1:2], None, ALU.mult)
                V.tensor_copy(zT[64:96, :], bank[64:96, 0:T])
                V.tensor_scalar(g_i[0:BH, :], bank[0:BH, T:2 * T], bg[:, l, 0:1], None, ALU.add).then_inc(free, 1)
                bank, free = tr_item("lf", l)
                V.tensor_scalar(g_f[0:BH, :], bank[0:BH, 0:T], bg[:, l, 1:2], None, ALU.add).then_inc(free, 1)
                ve.wait_ge(*tr_done("lf", l))
                V.scalar_tensor_tensor(g_n[0:BH, :], g_f[0:BH, :], -1.0, g_f[0:BH, :], ALU.mult,
                                       ALU.min).then_inc(gate_in, 1)
                ada(ADA_MIXER[l][0])
                negmaxes("a", 0, 1)
                for p in range(3):
                    bank, free = pj_item(f"uk{p}")
                    V.tensor_copy(kall[0:CN, 2 * p:2 * p + 2, :],
                                  bank[0:CN, :].rearrange("p (a t) -> p a t", a=2)).then_inc(free, 1)
                for b in range(TB):
                    bank, free = pj_item(f"uv{b}")
                    V.tensor_copy(vc[:, b, :], bank[:, 0:CH * CV]).then_inc(free, 1)
                negmaxes("a", 2, 3)
                ve.wait_ge(gate_ln, l + 1)
                G = slice(0, BH)
                zero = scr[G, 7, :]
                mark(V.scalar_tensor_tensor(g_f[G, :], g_f[G, :], 0.0, g_e[G, :], ALU.min, ALU.subtract))
                settle()
                mark(V.tensor_tensor_scan(g_b[G, :], g_f[G, :], zero, 0.0, ALU.add, ALU.add))
                settle()
                mark(V.tensor_tensor(g_a[G, :], g_i[G, :], g_b[G, :], ALU.subtract))
                settle()
                mark(V.tensor_tensor_scan(g_m[G, :], g_a[G, :], zero, 0.0, ALU.max, ALU.max))
                settle()
                mark(V.scalar_tensor_tensor(g_b[G, :], g_b[G, :], -1.0, g_m[G, :], ALU.mult, ALU.subtract))
                settle()
                V.tensor_scalar(g_m[G, :], g_m[G, :], -1.0, None, ALU.mult).then_inc(gates_ready, 1)
                negmaxes("a", 4, 5, 6, 7)
                combine(0)
                combine(1)
                ve.wait_ge(qcos_ready, 2 * (l + 1))
                R = slice(CN, CN + CR)
                for i in range(4):
                    name = (("rot", i), l)
                    ve.wait_ge(sc_full, SC.full(name))
                    nh = 2 if i < 3 else 1
                    bank = sc[SC.bank(name)][R, 0:nh * T].rearrange("p (a t) -> p a t", a=nh)
                    mark(V.tensor_tensor(bank, bank, sin[R, :].rearrange("p (o t) -> p o t", o=1).to_broadcast([CR, nh, T]),
                                         ALU.mult))
                    settle()
                    dst = qall[R, 2 * i:2 * i + 2, :] if i < 3 else kro[R, :].rearrange("p (o t) -> p o t", o=1)
                    V.tensor_tensor(dst, bank, qcos[R, 2 * i:2 * i + nh, :], ALU.add).then_inc(sc_free[SC.bank(name)], 1)
                for i in range(3):
                    ve.wait_ge(*pj_done(f"qk{i}", l))
                settle()
                for i in range(6):
                    mark(V.tensor_scalar(cv[:, i, :], raw[:, i, CW - 1:CW - 1 + T], wc[:, l, CW - 1, i:i + 1],
                                         bc[:, l, i:i + 1], ALU.mult, ALU.add))
                for j in range(CW - 2, -1, -1):
                    settle()
                    for i in range(6):
                        last = V.scalar_tensor_tensor(cv[:, i, :], raw[:, i, j:j + T], wc[:, l, j, i:i + 1], cv[:, i, :],
                                                      ALU.mult, ALU.add)
                        if j or i < 5:
                            mark(last)
                last.then_inc(conv_ready, 1)
                ada(ADA_MIXER[l][1])
                combine(2)
                combine(3)
                negmaxes("c", 0, 1, 2, 3)
                for b in range(TB):
                    bank, free = pj_item(f"vb{b}")
                    V.tensor_copy(vbx[:, b, :, 0:BD], bank[:, 0:BH * BD].rearrange("p (h d) -> p h d", h=BH)).then_inc(free, 1)
                ve.wait_ge(ao_sq, l + 1)
                mark(V.tensor_reduce(red[:, 0:8], sqj[:, 0:8 * AV].rearrange("p (a d) -> p a d", d=AV), AX.X, ALU.add))
                settle()
                V.tensor_scalar(ms[:, MS[("a", l)], 0:8], red[:, 0:8], 1.0 / AV, EPS, ALU.mult, ALU.add).then_inc(mean_ready, 1)
                negmaxes("c", 4)
                r = root(("a", l))[:, 0:8].rearrange("p (b h o) -> p b h o", b=TB, o=1).to_broadcast([P, TB, AH, AV])
                bank, free = tr_item("ao", l)
                V.tensor_tensor(tok[:, :, 0:AH * AV].rearrange("p b (h d) -> p b h d", h=AH),
                                bank.rearrange("p (b h d) -> p b h d", b=TB, h=AH), r, ALU.mult).then_inc(free, 1)

                def pt(u):
                    p, b = u // 2, u % 2
                    bank, free = tr_item(f"pt{u}", l)
                    o, n = 2 * b * P, 2 * (b + 1) * P
                    V.tensor_copy(PT[:, p, o:o + n], bank[:, 0:n]).then_inc(free, 1)

                pt(1)
                negmaxes("c", 5)
                pt(3)
                pt(5)
                mark(V.reciprocal(rc[:, 8:14, :], se[:, 8:14, :]))
                for h in range(BH):
                    name = (("s", h), l)
                    ve.wait_ge(sc_full, SC.full(name))
                    ve.wait_ge(*sc_done("w", h, l))
                    V.scalar_tensor_tensor(scw[:, h, :], sc[SC.bank(name)][:, 0:3 * P], SC_B, W[:, h % 2, :],
                                           ALU.mult, ALU.mult).then_inc(sc_free[SC.bank(name)], 1)
                ada(ADA_MIXER[l][2])
                settle()
                for b in range(TB):
                    bank, free = tr_item(f"co{b}", l)
                    r = rc[:, 8:14, :].rearrange("p (q b) j -> p b q j", b=TB)[:, b, :, :]
                    r = r.rearrange("p q (j o) -> p q j o", o=1).to_broadcast([P, 3, 2, CV])
                    o = tok[:, b, D - CH * CV:D].rearrange("p (q j d) -> p q j d", q=3, j=2)
                    V.tensor_tensor(o, bank[:, 0:CH * CV].rearrange("p (q j d) -> p q j d", q=3, j=2), r,
                                    ALU.mult).then_inc(free, 1)
                bo = []
                for b in range(TB):
                    bank, free = tr_item(f"bo{b}", l)
                    bank = bank[:, 0:BH * (BD + 1)].rearrange("p (h d) -> p h d", h=BH)
                    bo.append((bank, free))
                    mark(V.tensor_copy(den[:, b * BH:(b + 1) * BH].rearrange("p (h o) -> p h o", o=1),
                                       bank[:, :, BD:BD + 1]))
                settle()
                ve.wait_ge(*tr_done("gt", l))
                mark(V.scalar_tensor_tensor(rden[:, :], den[:, :], -1.0, den[:, :], ALU.mult, ALU.max))
                settle()
                mark(V.tensor_tensor(den[:, :], rden[:, :], em[:, :], ALU.max))
                settle()
                mark(V.reciprocal(rden[:, :], den[:, :]))
                settle()
                for b, (bank, free) in enumerate(bo):
                    r = rden[:, b * BH:(b + 1) * BH].rearrange("p (h o) -> p h o", o=1).to_broadcast([P, BH, BD])
                    V.tensor_tensor(hb[:, b * BH:(b + 1) * BH, :], bank[:, :, 0:BD], r, ALU.mult).then_inc(free, 1)
                ve.wait_ge(hb_sq, l + 1)
                mark(V.tensor_reduce(red[:, :], sqj[:, :].rearrange("p (a d) -> p a d", d=BD), AX.X, ALU.add))
                settle()
                V.tensor_scalar(ms[:, MS[("b", l)], 0:12], red[:, :], 1.0 / BD, EPS, ALU.mult, ALU.add).then_inc(mean_ready, 1)
                r = root(("b", l)).rearrange("p (b h o) -> p b h o", b=TB, o=1).to_broadcast([P, TB, BH, BD])
                V.tensor_tensor(tok[:, :, AH * AV:AH * AV + BH * BD].rearrange("p b (h d) -> p b h d", h=BH),
                                hb.rearrange("p (b h) d -> p b h d", b=TB), r, ALU.mult).then_inc(tok_ready, 1)
                ve.wait_ge(obt_ready, l + 1)
                bank, free = tr_item("mt1", l)
                for j in range(2):
                    last = V.scalar_tensor_tensor(mixT[:, 2 + j, :], bank[:, j * T:(j + 1) * T], gml[:, l, j:j + 1],
                                                  obt[:, j, :], ALU.mult, ALU.mult)
                last.then_inc(free, 1)
                bank, free = tr_item("mt2", l)
                V.scalar_tensor_tensor(mixT[:, 4, :], bank[:, 0:T], gml[:, l, 2:3], obt[:, 2, :], ALU.mult, ALU.mult)
                V.tensor_copy(mixT[:, 5, :], bank[:, T:2 * T]).then_inc(free, 1)
                ada(ADA_MIXER[l][3])

            mean("pre", 0)
            ve.wait_ge(param_in, 16 * n_param)
            for i in range(2):
                V.tensor_tensor(lam_pr[:, i, :], lam_in[:, i, :], lam_in[:, 2 + i, :], ALU.mult).then_inc(lam_prod, 1)
            bank, free = tr_item("param1")
            V.tensor_copy(pcol[:, 0, 0:124], bank[:, 0:124]).then_inc(free, 1)
            bank, free = tr_item("param2")
            V.tensor_copy(pcol[:, 1, 0:112], bank[:, 0:112]).then_inc(free, 1)
            for l in range(L):
                mark(V.tensor_scalar(gd[:, l:l + 1], gdr[:, l:l + 1], 1.0 - LAM0[l], None, ALU.mult))
                mark(V.memset(lam_v[:, l, 0:1], 1.0))
            R = slice(CN, CN + CR)
            ang, k_f, k_i = E[R, 0, 0:T], E[R, 1, 0:T], E[R, 2, 0:T].bitcast(I32)
            s_, c_, w_ = sin[R, :], cos[R, :], E[R, 3, 0:T]
            mark(V.tensor_copy(ang, posi[R, :]))
            settle()
            mark(V.tensor_scalar(ang, ang, con[R, C_FREQ:C_FREQ + 1], None, ALU.mult))
            settle()
            mark(V.tensor_scalar(k_i, ang, 1.0 / TWO_PI, None, ALU.mult))
            settle()
            mark(V.tensor_copy(k_f, k_i))
            settle()
            for part in (PI_1, PI_2, PI_3):
                mark(V.scalar_tensor_tensor(ang, k_f, -part, ang, ALU.mult, ALU.add))
                settle()

            def wrap(x):
                mark(V.tensor_scalar(w_, x, PI_LOW, -TWO_PI, ALU.is_gt, ALU.mult))
                settle()
                mark(V.tensor_tensor(x, x, w_, ALU.add))
                settle()

            wrap(ang)
            mark(V.tensor_scalar(c_, ang, np.pi / 2, None, ALU.add))
            settle()
            wrap(c_)
            V.tensor_scalar(s_, ang, -PI_LOW, PI_LOW, ALU.max, ALU.min).then_inc(rope_in, 1)
            V.tensor_scalar(c_, c_, -PI_LOW, PI_LOW, ALU.max, ALU.min).then_inc(rope_in, 1)
            ve.wait_ge(*tr_done("lam"))
            for l in range(L):
                mark(V.tensor_tensor(lam_v[:, l, 1:2], lam_e[:, 1, l:l + 1], lam_e[:, 0, l:l + 1], ALU.subtract))
            settle()
            for l in range(L):
                mark(V.tensor_scalar(lam_v[:, l, 1:2], lam_v[:, l, 1:2], -LAM0[l], None, ALU.add))
            ve.wait_ge(*tr_done("param2"))
            for third in ADA_START:
                ada(third)
            ve.wait_ge(y_quarter, 4)
            settle()
            pre(0)
            mixer(0)
            post(0)
            pre(1)
            for t in range(FT):
                ve.wait_ge(silu_done, t + 1)
                if t >= 2:
                    ve.wait_ge(down_done, t - 1)
                V.tensor_tensor(act[:, t % 2, :], PG[:, t % 2, T:2 * T], sg[:, t % 2, :], ALU.mult).then_inc(act_ready, 1)
                if t == 3:
                    ada(ADA_DENSE)
            post(1)
            pre(2)
            mixer(1)
            post(2)
            pre(3)

            bank, free = tr_item("router")
            V.tensor_tensor(lg, bank[:, 0:TB * NE].rearrange("p (b e) -> p b e", b=TB),
                            rbias[:, :].rearrange("p (o e) -> p o e", o=1).to_broadcast([P, TB, NE]), ALU.add).then_inc(free, 1)
            ve.wait_ge(*tr_done("router"))
            for b in range(TB):
                mark(V.max(mx8[:, b, :], lg[:, b, :]))
            settle()
            for b in range(TB):
                mark(V.max_index(ix8[:, b, :], mx8[:, b, :], lg[:, b, :]))
            V.tensor_tensor(gt2[:, :, 0:1], mx8[:, :, 1:2], mx8[:, :, 0:1], ALU.subtract).then_inc(gap_ready, 1)
            settle()
            mark(V.tensor_copy(ixf, ix8[:, :, :]))
            ve.wait_ge(gap_exp, 1)
            mark(V.tensor_scalar(gt2[:, :, 2:3], gt2[:, :, 1:2], 1.0, None, ALU.add))
            settle()
            mark(V.reciprocal(gt2[:, :, 0:1], gt2[:, :, 2:3]))
            settle()
            mark(V.tensor_tensor(gt2[:, :, 3:4], gt2[:, :, 1:2], gt2[:, :, 0:1], ALU.mult))
            settle()
            for b in range(TB):
                mark(V.tensor_scalar(oh1[:, b, :], iota[:, 0:NE], ixf[:, b, 0:1], None, ALU.is_equal))
                mark(V.tensor_scalar(oh2[:, b, :], iota[:, 0:NE], ixf[:, b, 1:2], None, ALU.is_equal))
            settle()
            for b in range(TB):
                mark(V.tensor_scalar(Gm[:, b, 0:NE], oh1[:, b, :], gt2[:, b, 0:1], None, ALU.mult))
            settle()
            for b in range(TB):
                mark(V.scalar_tensor_tensor(Gm[:, b, 0:NE], oh2[:, b, :], gt2[:, b, 3:4], Gm[:, b, 0:NE], ALU.mult, ALU.add))
            for x in (Gm, Mm, pos):
                mark(V.memset(x[:, :, NE:NE + 1], 0.0))
            V.tensor_tensor(Mm[:, :, 0:NE], oh1, oh2, ALU.add).then_inc(routed, 1)
            bank, free = tr_item("rank")
            V.tensor_copy(pos[:, :, 0:NE], bank[:, 0:TB * NE].rearrange("p (b e) -> p b e", b=TB))
            V.tensor_copy(cnt[:, :], bank[:, 2 * NE:3 * NE]).then_inc(free, 1)
            ve.wait_ge(*tr_done("rank"))
            settle()
            ve.wait_ge(routed, 1)
            ve.wait_ge(yacc_zero, 1)

            def one_hot(e):
                for b in range(TB):
                    V.tensor_scalar(oh[:, b, :], iota, pos[:, b, bass.ds(e, 1)], Mm[:, b, bass.ds(e, 1)],
                                    ALU.is_equal, ALU.mult)
                    last = V.tensor_scalar(ohg[:, b, :], iota, pos[:, b, bass.ds(e, 1)], Gm[:, b, bass.ds(e, 1)],
                                           ALU.is_equal, ALU.mult)
                last.then_inc(hot_ready, 1)

            one_hot(0)
            with ve.Fori(0, NE) as e:
                n_tok = ve.value_load(cnt[0:1, bass.ds(e, 1)], min_val=0, max_val=T)
                def expert(n):
                    def item(i):
                        ve.wait_ge(ax_full, e * AX_T + (i + 1))
                        return ax_banks[AX_BANK[i]], ax_free[AX_BANK[i]]

                    for i in (1, 3):
                        bank, free = item(i)
                        V.tensor_copy(mixT[:, 2 * i:2 * i + 2, 0:n],
                                      bank.rearrange("p (a t) -> p a t", a=2)[:, :, 0:n]).then_inc(free, 1)
                    bank, free = item(5)
                    for j, m in blocks(n):
                        last = V.tensor_copy(gPT[0:m, j, P:2 * P], bank[0:m, j * P:(j + 1) * P])
                    last.then_inc(free, 1)
                    one_hot(e + 1)
                    us = units(n)
                    step = 2 // len(blocks(n))
                    for u, s, j, m in us:
                        gate, up, r, width = gate_up_of(m, u)
                        ve.wait_ge(silu_done, at_unit(e, n, u))
                        V.tensor_tensor(actK[r, u % 2, 0:width], up, sgK[r, u % 2, 0:width],
                                        ALU.mult).then_inc(act_ready, step)
                        ve.wait_ge(tp_full, at_own(e, n, u))
                        if u >= 2:
                            ve.wait_ge(down_done, at_unit(e, n, u - 2))
                        V.tensor_copy(actT[:, u % 2, :, 0:m], turned_of(m, u)).then_inc(at_ready, step)
                    ve.wait_ge(down_done, e * FT + 2 * FT)
                    for j, m in blocks(n):
                        for piece, c, width in outputs(j, m):
                            if c >= D // 2:
                                last = V.tensor_copy(yeK[0:m, j, c:c + width], piece)
                    last.then_inc(ye_ready, 1)
                    for i in range(6, 10):
                        bank, free = item(i)
                        o = yacc[:, 2 * (i - 6):2 * (i - 6) + 2, :]
                        V.tensor_tensor(o, o, bank.rearrange("p (a t) -> p a t", a=2), ALU.add).then_inc(free, 1)

                variants(ve, n_tok, expert)
            for b in range(4):
                ve.wait_ge(ax_free[b], (NE + 1) * AX_F[b])
            ve.sem_inc(yacc_ready, 4 * NE)
            post(3)

        @block.gpsimd
        def _(po):
            G = nc.gpsimd

            def roots(name, n):
                G.tensor_tensor(rs[:, MS[name], 0:n], ms[:, MS[name], 0:n], half[:, 0:n], ALU.pow).then_inc(rstd_ready, 1)

            def norm_roots(kind, n):
                po.wait_ge(*tr_done(kind, n, "total"))
                G.tensor_tensor(root_[:, :], meps[:, :], half[:, 0:TB], ALU.pow).then_inc(rstd_ready, 1)

            def update(n):
                for k in range(KD // 2):
                    po.wait_ge(upd_ready, KD * n + k + 1)
                    G.tensor_tensor(xT[:, k, :], xT[:, k, :], scr[:, k, :], ALU.add).then_inc(x_upd, 1)

            def mixer(l):
                for b in range(TB):
                    po.wait_ge(*pj_done(f"lat{b}", l))
                G.tensor_copy(latn[:, :, 320:352], lat[:, :, LATW - CR:LATW]).then_inc(kr_ready, 1)
                po.wait_ge(mean_ready, 3 * l + 1)
                po.wait_ge(kr_ready, l + 1)
                roots(("c", l), 4)
                R = slice(CN, CN + CR)
                cs = cos[R, :].rearrange("p (o t) -> p o t", o=1)
                po.wait_ge(*pj_done("uq1", l))
                po.wait_ge(*pj_done("uq2", l))
                po.wait_ge(rope_set, 2)
                po.wait_ge(rstd_ready, RS[("c", l)] + 1)
                G.tensor_tensor(qcos[R, 0:CH, :], qall[R, :, :], cs.to_broadcast([CR, CH, T]), ALU.mult).then_inc(qcos_ready, 1)
                G.tensor_tensor(qcos[R, CH, :], zT[R, :], cos[R, :], ALU.mult).then_inc(qcos_ready, 1)
                po.wait_ge(*sc_done("rot", 3, l))
                po.wait_ge(qcos_ready, 2 * (l + 1))
                G.tensor_copy(kall[R, :, :], kro[R, :].rearrange("p (o t) -> p o t", o=1).to_broadcast([CR, CH, T])).then_inc(rope_done, 1)
                po.wait_ge(obt_tanh, l + 1)
                po.wait_ge(rope_done, l + 1)
                G.tensor_scalar(obt, obt, 1.0, 0.5, ALU.add, ALU.mult).then_inc(obt_ready, 1)
                po.wait_ge(mean_ready, 3 * l + 2)
                roots(("a", l), 8)
                po.wait_ge(mean_ready, 3 * l + 3)
                roots(("b", l), 12)

            G.memset(ones[:, :], 1.0).then_inc(const_set, 1)
            G.memset(half[:, :], -0.5).then_inc(const_set, 1)
            G.memset(ccol[:, :, :], 0.0).then_inc(const_set, 1)
            po.wait_ge(const_set, 3)
            for l in range(L):
                norm_roots("pre", 2 * l)
                mixer(l)
                norm_roots("post", 2 * l)
                update(2 * l)
                norm_roots("pre", 2 * l + 1)
                if l == 1:
                    G.memset(yacc, 0.0).then_inc(yacc_zero, 1)
                norm_roots("post", 2 * l + 1)
                update(2 * l + 1)


_INS = ["x", "c", "positions", "w_ada", "b_ada", "g_norm", "w_in", "w_out", "lam_q1", "lam_k1", "lam_q2", "lam_k2",
        "g_diff", "w_conv", "b_conv", "b_igate", "b_fgate", "g_mlstm", "g_q_lat", "g_kv_lat", "w_uq", "w_ukv",
        "w_gate_d", "w_up_d", "w_down_d", "w_router", "b_router", "w_gate_e", "w_up_e", "w_down_e"]


def kernel(**inputs):
    import concourse.bacc as _bacc
    from concourse.bass_utils import run_bass_kernel_spmd as _run

    nc = _bacc.Bacc("TRN2", target_bir_lowering=False, num_devices=1)
    arrays, aps = {}, {}
    for name in _INS + ["consts"]:
        a = const_table() if name == "consts" else np.ascontiguousarray(inputs[name])
        arrays[f"in_{name}"] = a
        aps[name] = nc.dram_tensor(f"in_{name}", a.shape, mybir.dt.from_np(a.dtype), kind="ExternalInput").ap()
    result = nc.dram_tensor("result", (1, T, D), F32, kind="ExternalOutput").ap()
    build(nc, aps, result)
    r = _run(nc, [arrays], core_ids=[0])
    return r.results[0]["result"]
```
